# Optimizing a Trainium2 kernel written in Bass

```python
import jax, jax.numpy as jnp
from jax import lax
import numpy as np

D_MODEL = 1024
BATCH = 1
SEQ = 1024
DEPTH = 1

HEAD_DIM = 64
Q_BLOCK = 128
NSA_HEADS = 8
NSA_KV = 1
NSA_GROUP = NSA_HEADS // NSA_KV
CMP_STRIDE = 16
CMP_LEN = 2 * CMP_STRIDE
CMP_HID = 256
SEL_BLOCK = 64
SEL_TOPK = 8
NSA_WINDOW = 512
SB_HEADS = 4
SWA_HEADS = 4
SWA_KV = 2
SWA_GROUP = SWA_HEADS // SWA_KV
SWA_WINDOW = 128
N_EXPERTS = 16
N_GROUPS = 4
EXPERTS_PER_GROUP = N_EXPERTS // N_GROUPS
TOP_K = 2
D_EXPERT = D_MODEL // 2
MOE_BLOCK = 512
N_BRANCH = 3
EPS = 1e-6
NEG = -1e30
BIG = 1e30

A_WIDTH = NSA_HEADS * HEAD_DIM
B_WIDTH = SB_HEADS * HEAD_DIM
C_WIDTH = SWA_HEADS * HEAD_DIM
IN_WIDTHS = (A_WIDTH, 6 * NSA_KV * HEAD_DIM, 3 * NSA_HEADS, 3 * B_WIDTH, C_WIDTH, 2 * SWA_KV * HEAD_DIM, N_BRANCH * D_MODEL)
N_IN = sum(IN_WIDTHS)

kernel_name = "hybrid_nsa_stickbreak_swa_moe"

f32 = jnp.float32

def rmsnorm(x, g):
    xf = x.astype(f32)
    y = xf * lax.rsqrt(jnp.mean(xf * xf, axis=-1, keepdims=True) + EPS)
    return (y * g.astype(f32)).astype(x.dtype)

def alibi_slopes(n):
    return 2.0 ** (-8.0 * jnp.arange(1, n + 1, dtype=f32) / n)

def masked_softmax(s, mask):
    s = jnp.where(mask, s, NEG)
    m = jnp.max(s, axis=-1, keepdims=True)
    p = jnp.where(mask, jnp.exp(s - m), 0.0)
    return p / jnp.maximum(jnp.sum(p, axis=-1, keepdims=True), 1e-30)

def split_cols(z, widths):
    return jnp.split(z, np.cumsum(widths)[:-1].tolist(), axis=-1)

def nsa_compress(k, pe, w1, w2):
    B, S, G, HD = k.shape
    ch = k.reshape(B, S // CMP_STRIDE, CMP_STRIDE, G, HD)
    blk = jnp.concatenate([ch[:, :-1], ch[:, 1:]], axis=2) + pe[None, None, :, None, :]
    flat = jnp.transpose(blk, (0, 1, 3, 2, 4)).reshape(B, S // CMP_STRIDE - 1, G, CMP_LEN * HD)
    return jax.nn.gelu(flat @ w1) @ w2

def nsa_attention(q, kv, gates, cmp_pe_k, cmp_w1_k, cmp_w2_k, cmp_pe_v, cmp_w1_v, cmp_w2_v, q_gain, k_gain, slopes):
    B, S, G, HG, HD = q.shape
    NB = S // Q_BLOCK
    NC = S // CMP_STRIDE - 1
    NSEL = S // SEL_BLOCK
    KSEL = min(SEL_TOPK, NSEL)
    R = SEL_BLOCK // CMP_STRIDE
    scale = HD ** -0.5
    q = rmsnorm(q, q_gain)
    k_cmp = rmsnorm(nsa_compress(kv[:, :, 0], cmp_pe_k, cmp_w1_k, cmp_w2_k), k_gain[0])
    v_cmp = nsa_compress(kv[:, :, 1], cmp_pe_v, cmp_w1_v, cmp_w2_v)
    k_slc = jnp.transpose(rmsnorm(kv[:, :, 2], k_gain[1]), (0, 2, 1, 3))
    v_slc = jnp.transpose(kv[:, :, 3], (0, 2, 1, 3))
    pad = ((0, 0), (NSA_WINDOW, 0), (0, 0), (0, 0))
    k_win = jnp.pad(rmsnorm(kv[:, :, 4], k_gain[2]), pad)
    v_win = jnp.pad(kv[:, :, 5], pad)
    c_end = jnp.arange(NC) * CMP_STRIDE + (CMP_LEN - 1)
    blk_ids = jnp.arange(NSEL)
    ov_w = (0.5,) + (1.0,) * (R - 1) + (0.5,)
    alibi = slopes.astype(f32)[None, :, :, None, None]
    gather = jax.vmap(jax.vmap(lambda src, idx: src[idx]))

    def one_block(args):
        n, qb, gb = args
        t = n * Q_BLOCK + jnp.arange(Q_BLOCK)
        s = jnp.einsum('bqghd,bcgd->bghqc', qb, k_cmp, preferred_element_type=f32) * scale
        dist = (t[:, None] - c_end[None, :]).astype(f32)
        p_cmp = masked_softmax(s - alibi * dist, dist >= 0)
        o_cmp = jnp.einsum('bghqc,bcgd->bqghd', p_cmp.astype(v_cmp.dtype), v_cmp)
        imp = jnp.pad(p_cmp.sum(axis=2), ((0, 0), (0, 0), (0, 0), (1, R * NSEL - NC)))
        imp = sum(w * imp[..., r: r + R * NSEL: R] for r, w in enumerate(ov_w))
        cur = (t // SEL_BLOCK)[:, None]
        forced = (blk_ids == 0) | (blk_ids == cur) | (blk_ids == cur - 1)
        score = jnp.where(blk_ids <= cur, jnp.where(forced, BIG, imp), -jnp.inf)
        _, sel = lax.top_k(score, KSEL)
        tok = (sel[..., None] * SEL_BLOCK + jnp.arange(SEL_BLOCK)).reshape(B, G, Q_BLOCK, KSEL * SEL_BLOCK)
        ks = gather(k_slc, tok)
        vs = gather(v_slc, tok)
        s = jnp.einsum('bqghd,bgqtd->bghqt', qb, ks, preferred_element_type=f32) * scale
        dist = (t[:, None] - tok).astype(f32)[:, :, None]
        p = masked_softmax(s - alibi * dist, dist >= 0)
        o_slc = jnp.einsum('bghqt,bgqtd->bqghd', p.astype(vs.dtype), vs)
        kw = lax.dynamic_slice_in_dim(k_win, n * Q_BLOCK, Q_BLOCK + NSA_WINDOW, axis=1)
        vw = lax.dynamic_slice_in_dim(v_win, n * Q_BLOCK, Q_BLOCK + NSA_WINDOW, axis=1)
        pos = n * Q_BLOCK - NSA_WINDOW + jnp.arange(Q_BLOCK + NSA_WINDOW)
        dist = (t[:, None] - pos[None, :]).astype(f32)
        mask = (dist >= 0) & (dist < NSA_WINDOW) & (pos[None, :] >= 0)
        s = jnp.einsum('bqghd,bkgd->bghqk', qb, kw, preferred_element_type=f32) * scale
        p = masked_softmax(s - alibi * dist, mask)
        o_win = jnp.einsum('bghqk,bkgd->bqghd', p.astype(vw.dtype), vw)
        return gb[..., 0:1] * o_cmp + gb[..., 1:2] * o_slc + gb[..., 2:3] * o_win

    to_blocks = lambda z: jnp.swapaxes(z.reshape(B, NB, Q_BLOCK, *z.shape[2:]), 0, 1)
    o = lax.map(one_block, (jnp.arange(NB), to_blocks(q), to_blocks(gates)))
    return jnp.swapaxes(o, 0, 1).reshape(B, S, G * HG * HD)

def stick_breaking(q, k, v):
    B, S, H, HD = q.shape
    NB = S // Q_BLOCK
    q = q * HD ** -0.5
    j = jnp.arange(Q_BLOCK)
    tri_incl = (j[:, None] >= j[None, :]).astype(f32)
    outs = []
    for n in range(NB):
        L = (n + 1) * Q_BLOCK
        z = jnp.einsum('bqhd,bshd->bhqs', q[:, n * Q_BLOCK:L], k[:, :L], preferred_element_type=f32)
        mask = jnp.arange(L)[None, :] < (n * Q_BLOCK + j)[:, None]
        lk = jnp.where(mask, -jax.nn.softplus(z), 0.0).reshape(B, H, Q_BLOCK, n + 1, Q_BLOCK)
        within = jnp.einsum('bhqcj,js->bhqcs', lk, tri_incl)
        cb = jnp.arange(n + 1)
        later = jnp.einsum('bhqc,cd->bhqd', lk.sum(axis=-1), (cb[:, None] > cb[None, :]).astype(f32))
        r = (within + later[..., None]).reshape(B, H, Q_BLOCK, L)
        a = jnp.where(mask, jnp.exp(z + r), 0.0)
        outs.append(jnp.einsum('bhqs,bshd->bqhd', a.astype(v.dtype), v[:, :L]))
    return jnp.concatenate(outs, axis=1).reshape(B, S, H * HD)

def swa_with_sinks(q, k, v, sinks, slopes):
    B, S, G, HG, HD = q.shape
    NB = S // Q_BLOCK
    qb = q.reshape(B, NB, Q_BLOCK, G, HG, HD)

    def band(z):
        zp = jnp.pad(z, ((0, 0), (Q_BLOCK, 0), (0, 0), (0, 0))).reshape(B, NB + 1, Q_BLOCK, G, HD)
        return jnp.concatenate([zp[:, :-1], zp[:, 1:]], axis=2)

    kb, vb = band(k), band(v)
    r = jnp.arange(2 * Q_BLOCK)
    dist = Q_BLOCK + jnp.arange(Q_BLOCK)[:, None] - r[None, :]
    key_pos = (jnp.arange(NB) * Q_BLOCK - Q_BLOCK)[:, None] + r[None, :]
    mask = ((dist >= 0) & (dist < SWA_WINDOW))[None] & (key_pos >= 0)[:, None, :]
    mask = mask[None, :, None, None]
    s = jnp.einsum('bnqghd,bnkgd->bnghqk', qb, kb, preferred_element_type=f32) * HD ** -0.5
    s = jnp.where(mask, s - slopes.astype(f32)[:, :, None, None] * dist.astype(f32), NEG)
    sink = sinks.astype(f32)[:, :, None, None]
    m = jnp.maximum(jnp.max(s, axis=-1, keepdims=True), sink)
    p = jnp.where(mask, jnp.exp(s - m), 0.0)
    p = p / (jnp.sum(p, axis=-1, keepdims=True) + jnp.exp(sink - m))
    o = jnp.einsum('bnghqk,bnkgd->bnqghd', p.astype(vb.dtype), vb)
    return o.reshape(B, S, G * HG * HD)

def hybrid_mixer(h, w_in, cmp_pe_k, cmp_w1_k, cmp_w2_k, cmp_pe_v, cmp_w1_v, cmp_w2_v, nsa_q_gain, nsa_k_gain,
                 swa_q_gain, swa_k_gain, swa_sinks, w_branch_a, w_branch_b, w_branch_c, w_out, nsa_slopes, swa_slopes):
    B, S, D = h.shape
    q_a, kv_a, gate_a, qkv_b, q_c, kv_c, merge = split_cols(h @ w_in, IN_WIDTHS)
    o_a = nsa_attention(q_a.reshape(B, S, NSA_KV, NSA_GROUP, HEAD_DIM),
                        kv_a.reshape(B, S, 6, NSA_KV, HEAD_DIM),
                        jax.nn.sigmoid(gate_a).reshape(B, S, NSA_KV, NSA_GROUP, 3),
                        cmp_pe_k, cmp_w1_k, cmp_w2_k, cmp_pe_v, cmp_w1_v, cmp_w2_v,
                        nsa_q_gain, nsa_k_gain, nsa_slopes)
    qkv_b = qkv_b.reshape(B, S, 3, SB_HEADS, HEAD_DIM)
    o_b = stick_breaking(qkv_b[:, :, 0], qkv_b[:, :, 1], qkv_b[:, :, 2])
    kv_c = kv_c.reshape(B, S, 2, SWA_KV, HEAD_DIM)
    o_c = swa_with_sinks(rmsnorm(q_c.reshape(B, S, SWA_KV, SWA_GROUP, HEAD_DIM), swa_q_gain),
                         rmsnorm(kv_c[:, :, 0], swa_k_gain), kv_c[:, :, 1],
                         swa_sinks.reshape(SWA_KV, SWA_GROUP), swa_slopes)
    g = jax.nn.sigmoid(merge).reshape(B, S, N_BRANCH, D)
    y = g[:, :, 0] * (o_a @ w_branch_a) + g[:, :, 1] * (o_b @ w_branch_b) + g[:, :, 2] * (o_c @ w_branch_c)
    return y @ w_out

def grouped_moe(h, w_router, router_bias, w_gate, w_up, w_down):
    B, S, D = h.shape
    hf = h.reshape(-1, D)
    N = hf.shape[0]
    scores = jax.nn.sigmoid((hf @ w_router).astype(f32))
    sel = (scores + router_bias.astype(f32)).reshape(N, N_GROUPS, EXPERTS_PER_GROUP)
    grp_score = lax.top_k(sel, TOP_K)[0].sum(axis=-1)
    g_idx = jnp.argmax(grp_score, axis=-1)
    in_grp = jnp.take_along_axis(sel, g_idx[:, None, None], axis=1)[:, 0]
    _, e_local = lax.top_k(in_grp, TOP_K)
    e_idx = (g_idx[:, None] * EXPERTS_PER_GROUP + e_local).astype(jnp.int32)
    w = jnp.take_along_axis(scores, e_idx, axis=-1)
    w = w / jnp.sum(w, axis=-1, keepdims=True)
    NK = N * TOP_K
    n_blk = -(-NK // MOE_BLOCK) + N_EXPERTS
    flat_e = e_idx.reshape(-1)
    order = jnp.argsort(flat_e)
    e_sorted = flat_e[order]
    counts = jnp.bincount(flat_e, length=N_EXPERTS)
    padded = (counts + MOE_BLOCK - 1) // MOE_BLOCK * MOE_BLOCK
    p_end = jnp.cumsum(padded)
    p_start = p_end - padded
    start = jnp.cumsum(counts) - counts
    dest = p_start[e_sorted] + jnp.arange(NK) - start[e_sorted]
    slot_tok = jnp.full((n_blk * MOE_BLOCK,), N, jnp.int32).at[dest].set((order // TOP_K).astype(jnp.int32))
    slot_w = jnp.zeros((n_blk * MOE_BLOCK,), hf.dtype).at[dest].set(w.reshape(-1)[order].astype(hf.dtype))
    blk_e = jnp.minimum(jnp.searchsorted(p_end, jnp.arange(n_blk) * MOE_BLOCK, side='right'), N_EXPERTS - 1)
    xs = jnp.concatenate([hf, jnp.zeros((1, D), hf.dtype)], axis=0)[slot_tok].reshape(n_blk, MOE_BLOCK, D)
    a = jax.nn.silu(jnp.einsum('nrd,ndf->nrf', xs, w_gate[blk_e])) * jnp.einsum('nrd,ndf->nrf', xs, w_up[blk_e])
    y = jnp.einsum('nrf,nfd->nrd', a, w_down[blk_e]).reshape(-1, D) * slot_w[:, None]
    out = jnp.zeros((N + 1, D), hf.dtype).at[slot_tok].add(y)[:N]
    return out.reshape(B, S, D)

def setup_inputs(seed: int = 0) -> dict:
    key = jax.random.key(seed)
    ks = jax.random.split(key, 27)
    nrm = lambda k, shape, s: jax.random.normal(k, shape, f32) * s
    L, D, HD = DEPTH, D_MODEL, HEAD_DIM
    return {
        "x": nrm(ks[0], (BATCH, SEQ, D), 1.0),
        "c": nrm(ks[1], (BATCH, D), 1.0),
        "w_ada": nrm(ks[2], (L, D, 6 * D), 0.5 * D ** -0.5),
        "b_ada": nrm(ks[3], (L, 6 * D), 0.02),
        "g_norm_mix": 1.0 + nrm(ks[4], (L, D), 0.02),
        "g_norm_moe": 1.0 + nrm(ks[5], (L, D), 0.02),
        "w_in": nrm(ks[6], (L, D, N_IN), D ** -0.5),
        "cmp_pe_k": nrm(ks[7], (L, CMP_LEN, HD), 0.02),
        "cmp_w1_k": nrm(ks[8], (L, CMP_LEN * HD, CMP_HID), (CMP_LEN * HD) ** -0.5),
        "cmp_w2_k": nrm(ks[9], (L, CMP_HID, HD), CMP_HID ** -0.5),
        "cmp_pe_v": nrm(ks[10], (L, CMP_LEN, HD), 0.02),
        "cmp_w1_v": nrm(ks[11], (L, CMP_LEN * HD, CMP_HID), (CMP_LEN * HD) ** -0.5),
        "cmp_w2_v": nrm(ks[12], (L, CMP_HID, HD), CMP_HID ** -0.5),
        "nsa_q_gain": 1.0 + nrm(ks[13], (L, HD), 0.02),
        "nsa_k_gain": 1.0 + nrm(ks[14], (L, 3, HD), 0.02),
        "swa_q_gain": 1.0 + nrm(ks[15], (L, HD), 0.02),
        "swa_k_gain": 1.0 + nrm(ks[16], (L, HD), 0.02),
        "swa_sinks": nrm(ks[17], (L, SWA_HEADS), 1.0),
        "w_branch_a": nrm(ks[18], (L, A_WIDTH, D), A_WIDTH ** -0.5),
        "w_branch_b": nrm(ks[19], (L, B_WIDTH, D), B_WIDTH ** -0.5),
        "w_branch_c": nrm(ks[20], (L, C_WIDTH, D), C_WIDTH ** -0.5),
        "w_out": nrm(ks[21], (L, D, D), D ** -0.5),
        "w_router": nrm(ks[22], (D, N_EXPERTS), D ** -0.5),
        "router_bias": nrm(ks[23], (N_EXPERTS,), 0.01),
        "w_exp_gate": nrm(ks[24], (L, N_EXPERTS, D, D_EXPERT), D ** -0.5),
        "w_exp_up": nrm(ks[25], (L, N_EXPERTS, D, D_EXPERT), D ** -0.5),
        "w_exp_down": nrm(ks[26], (L, N_EXPERTS, D_EXPERT, D), D_EXPERT ** -0.5),
    }

def reference(x, c, w_ada, b_ada, g_norm_mix, g_norm_moe, w_in, cmp_pe_k, cmp_w1_k, cmp_w2_k, cmp_pe_v, cmp_w1_v,
              cmp_w2_v, nsa_q_gain, nsa_k_gain, swa_q_gain, swa_k_gain, swa_sinks, w_branch_a, w_branch_b,
              w_branch_c, w_out, w_router, router_bias, w_exp_gate, w_exp_up, w_exp_down):
    slopes = alibi_slopes(SWA_HEADS + NSA_HEADS)
    swa_slopes = slopes[:SWA_HEADS].reshape(SWA_KV, SWA_GROUP)
    nsa_slopes = slopes[SWA_HEADS:].reshape(NSA_KV, NSA_GROUP)
    cond = jax.nn.silu(c)
    for l in range(DEPTH):
        mod = cond @ w_ada[l] + b_ada[l]
        sh_a, sc_a, g_a, sh_m, sc_m, g_m = [m[:, None, :] for m in jnp.split(mod, 6, axis=-1)]
        h = rmsnorm(x, g_norm_mix[l]) * (1.0 + sc_a) + sh_a
        x = x + g_a * hybrid_mixer(h, w_in[l], cmp_pe_k[l], cmp_w1_k[l], cmp_w2_k[l], cmp_pe_v[l], cmp_w1_v[l],
                                   cmp_w2_v[l], nsa_q_gain[l], nsa_k_gain[l], swa_q_gain[l], swa_k_gain[l],
                                   swa_sinks[l], w_branch_a[l], w_branch_b[l], w_branch_c[l], w_out[l],
                                   nsa_slopes, swa_slopes)
        h = rmsnorm(x, g_norm_moe[l]) * (1.0 + sc_m) + sh_m
        x = x + g_m * grouped_moe(h, w_router, router_bias, w_exp_gate[l], w_exp_up[l], w_exp_down[l])
    return x


_drawn_inputs = setup_inputs


def setup_inputs(seed=0):
    import zlib

    import numpy as np

    out = dict(_drawn_inputs(seed))
    spreads = {}
    factors = {'g_norm_mix': 6.001,
     'g_norm_moe': 2.734,
     'cmp_pe_k': 8.0,
     'cmp_w2_k': 2.855,
     'cmp_pe_v': 8.0,
     'nsa_q_gain': 8.0,
     'nsa_k_gain': 8.0,
     'swa_q_gain': 6.429,
     'swa_k_gain': 6.577,
     'swa_sinks': 187.451}
    for name, (base, spread) in spreads.items():
        noise = np.random.default_rng([zlib.crc32(name.encode()), seed]).standard_normal(out[name].shape)
        drawn = base * np.exp(spread * noise) if base else spread * noise
        out[name] = __import__('jax').numpy.asarray(drawn.astype(out[name].dtype))
    for name, factor in factors.items():
        out[name] = (out[name] * factor).astype(out[name].dtype)
    return out
```

```python
from contextlib import ExitStack

import numpy as np
import concourse.bass as bass
from concourse import mybir

ALU = mybir.AluOpType
ACT = mybir.ActivationFunctionType
AX = mybir.AxisListType
F32 = mybir.dt.float32
F32R = mybir.dt.float32r
BF16 = mybir.dt.bfloat16
I32 = mybir.dt.int32
U32 = mybir.dt.uint32

P = 128
BANK = 512
HD = 64
EPS = 1e-6
MASKED = -1e30
NSA_H, SB_H, SWA_H = 8, 4, 4
CMP_STRIDE, CMP_LEN, CMP_HID = 16, 32, 256
SEL_BLOCK, SEL_TOPK, NSA_WINDOW = 64, 8, 512
N_GROUPS = 4
ROW_POS, ROW_SEL, AUG = 64, 96, 112
GELU_C = 1.5957691216057308
FORCE, TAKEN, TAKEN_MIN = 1e30, 3e30, 2.5e30
SLOT = 4096

NAMES = ("x", "c", "w_ada", "b_ada", "g_norm_mix", "g_norm_moe", "w_in", "cmp_pe_k", "cmp_w1_k", "cmp_w2_k", "cmp_pe_v",
         "cmp_w1_v", "cmp_w2_v", "nsa_q_gain", "nsa_k_gain", "swa_q_gain", "swa_k_gain", "swa_sinks", "w_branch_a",
         "w_branch_b", "w_branch_c", "w_out", "w_router", "router_bias", "w_exp_gate", "w_exp_up", "w_exp_down")


def alibi_slope(i):
    return float(2.0 ** (-8.0 * (i + 1) / (SWA_H + NSA_H)))


class Chain:

    def __init__(self, eng, sem):
        self.eng, self.sem, self.n = eng, sem, 0

    def __call__(self, ins):
        self.n += 1
        ins.then_inc(self.sem, 1)
        self.eng.wait_ge(self.sem, self.n)
        return ins


def hybrid_trunk(nc, x, c, w_ada, b_ada, g_norm_mix, g_norm_moe, w_in, cmp_pe_k, cmp_w1_k, cmp_w2_k, cmp_pe_v,
                 cmp_w1_v, cmp_w2_v, nsa_q_gain, nsa_k_gain, swa_q_gain, swa_k_gain, swa_sinks, w_branch_a,
                 w_branch_b, w_branch_c, w_out, w_router, router_bias, w_exp_gate, w_exp_up, w_exp_down, out):
    _, T, D = x.shape
    NT, NK = T // P, D // P
    NE, DE = w_exp_gate.shape[1], w_exp_gate.shape[3]
    A_W, B_W, C_W = NSA_H * HD, SB_H * HD, SWA_H * HD
    NC = T // CMP_STRIDE - 1
    NSEL = T // SEL_BLOCK
    C_Q, C_KV, C_GATE = 0, A_W, A_W + 6 * HD
    C_QB = C_GATE + 3 * NSA_H
    C_VB = C_QB + 2 * B_W
    C_QC = C_VB + B_W
    C_KC = C_QC + C_W
    C_MERGE = C_KC + C_W
    assert C_MERGE + 3 * D == w_in.shape[2]

    x2d = x.rearrange("b t d -> (b t) d")
    out2d = out.rearrange("b t d -> (b t) d")
    win = w_in.rearrange("l (k p) n -> p (l k) n", p=P)
    wada = w_ada.rearrange("l (k p) n -> p (l k) n", p=P)

    ctx = ExitStack()
    with ctx:
        def sb(name, shape, dt=F32):
            return ctx.enter_context(nc.sbuf_tensor(name, shape, dt))

        def twice(name, shape):
            with nc.sbuf_tensor(name, shape, F32) as a:
                pass
            return a, sb(name + "_r", shape, F32R)

        def sem(name):
            return ctx.enter_context(nc.semaphore(name))

        arena, arena_r = twice("arena", [P, 6 * SLOT])
        tmp = arena[:, 3 * SLOT:4 * SLOT]
        hT = arena[:, 4 * SLOT:6 * SLOT].rearrange("p (k t) -> p k t", k=NK)

        def slot(i, k=NK, w=None):
            a = arena[:, i * SLOT:(i + 1) * SLOT].rearrange("p (k n) -> p k n", k=k)
            return a if w is None else a[:, :, 0:w]

        heads = sb("heads", [P, NT * NK * P])
        qaT = heads[:, :].rearrange("p (n h t) -> p n h t", n=NT, h=NSA_H)
        kv, kv_r = twice("kv", [P, 6 * T])
        kslcT, kwinT = kv[:, 0:T], kv[:, T:2 * T]
        v_slc = kv[:, 2 * T:2 * T + NT * HD].rearrange("p (n d) -> p n d", n=NT)
        v_win = kv[:, 2 * T + NT * HD:3 * T].rearrange("p (n d) -> p n d", n=NT)
        v_b = kv[:, 3 * T:5 * T].rearrange("p (n d) -> p n d", n=NT)
        v_c = kv[:, 5 * T:6 * T].rearrange("p (n d) -> p n d", n=NT)
        bc = sb("bc", [P, 8 * T])
        qbT, kbT, qcT, kcT = (bc[:, 2 * T * i:2 * T * (i + 1)].rearrange("p (g t) -> p g t", g=2) for i in range(4))
        ga_bc, gm_bc = sb("ga_bc", [P, D]), sb("gm_bc", [P, D])
        cond_bc = gm_bc[:, :].rearrange("p (k m) -> p k m", k=NK)
        ident, identb = sb("ident", [P, P]), sb("identb", [P, P], BF16)
        tri_causal, tri_low, tri_strict = (sb(f"tri_{s}", [P, P], BF16) for s in ("causal", "low", "strict"))
        stair = sb("stair", [P, 120], BF16)
        swa_bias = sb("swa_bias", [P, SWA_H, 2 * P])
        force = sb("force", [P, NT, NSEL])
        gates = sb("gates", [P, NT, 3 * NSA_H])
        rows = sb("rows", [9 * NK, P])
        cols = sb("cols", [P, 9 * NK])
        mod = sb("mod", [P, 4 * NK])
        cond = sb("cond", [P, NK])
        pe_rows, peT = sb("pe_rows", [CMP_LEN, P]), sb("peT", [P, CMP_LEN])
        w2 = sb("w2", [P, 2, 2, HD])
        gain = sb("gain", [P, 8])
        st = sb("st", [P, 64])
        stp = sb("stp", [P, 32])
        kcmpT, v_cmp = sb("kcmpT", [ROW_SEL, 64]), sb("v_cmp", [P, 2 * HD])
        half = sb("half", [P, NSA_H])
        psum = ctx.enter_context(nc.psum_tensor("psum", [P, 8, BANK], F32))

        gain_q8, gain_sq8 = sb("gain_q8", [P, 1]), sb("gain_sq8", [P, 1])
        G_Q, G_KC, G_KS, G_KW, G_SQ, G_SK = (gain[:, i:i + 1] for i in range(6))
        SQ, SSX = 0, 16
        mod_a, mod_b = mod[:, 0:NK], mod[:, NK:2 * NK]
        mod_a2, mod_b2 = mod[:, 2 * NK:3 * NK], mod[:, 3 * NK:4 * NK]

        xt = [tmp[:, i * D:(i + 1) * D] for i in range(3)]
        tok = [tmp[:, i * 768:(i + 1) * 768] for i in range(2)]
        sq = tmp[:, 1536:2048]
        gm_bias = tmp[:, 3 * D:4 * D]
        kvcT = tmp[:, 2048:3072]
        blk = arena[:, 3 * SLOT:3 * SLOT + 2048].rearrange("p (l j) -> p l j", l=CMP_LEN)

        tmp_gh, tmp_ge = tmp[:, 2048:2304], tmp[:, 2304:2560]
        tmp_gv = tmp[:, 2560:2816].rearrange("p (c m) -> p c m", c=2)

        small_in, gain_in, x_in = sem("small_in"), sem("gain_in"), [sem(f"x_in{i}") for i in range(3)]
        w_in_slot = [sem(f"w_in_slot{i}") for i in range(3)]
        w_used = sem("w_used")
        tables = sem("tables")
        act_own, dve_own, pool_own = sem("act_own"), sem("dve_own"), sem("pool_own")
        rowsT, cond_e, cond_ok = sem("rowsT"), sem("cond_e"), sem("cond_ok")
        mod_ok = sem("mod_ok")
        x_sq, x_rstd, x_norm, xT_full, hT_dve, hT_act = (sem(s) for s in (
            "x_sq", "x_rstd", "x_norm", "xT_full", "hT_dve", "hT_act"))
        acc_full, acc_act, acc_dve = sem("acc_full"), sem("acc_act"), sem("acc_dve")
        squared, reduced, rstd_ok, tok_ok, tokT_full, tokT_dve, tokT_act = (sem(s) for s in (
            "squared", "reduced", "rstd_ok", "tok_ok", "tokT_full", "tokT_dve", "tokT_act"))
        blk_ok, hid_full, gelu_e, gelu_in, hid_ok, kcmp_full, kcmp_sq, kcmp_ms, kcmp_rstd, kcmp_tok, kcmpT_full, kcmp_ok = (
            sem(s) for s in ("blk_ok", "hid_full", "gelu_e", "gelu_in", "hid_ok", "kcmp_full", "kcmp_sq", "kcmp_ms",
                             "kcmp_rstd", "kcmp_tok", "kcmpT_full", "kcmp_ok"))
        mod2_ok = sem("mod2_ok")
        row_ok, turned = sem("row_ok"), sem("turned")

        def early_row(r):
            return bc[0:1, r % 2 * BANK:(r % 2 + 1) * BANK]

        def late_row(r):
            return tmp[0:1, r % 2 * BANK:(r % 2 + 1) * BANK]

        TOKCH = [(C_Q, A_W), (C_KV, 6 * HD + 3 * NSA_H), (C_VB, B_W + C_W), (C_KC, C_W)]
        loads = []
        for s in (1, 0):
            for h in range(2):
                loads.append([(slot, wada[:, :, s * D + h * BANK:s * D + (h + 1) * BANK])])
        for c0, w in TOKCH:
            loads.append([(lambda i, w=w: slot(i, w=w), win[:, :, c0:c0 + w])])
        loads.append([(slot, win[:, :, C_QB:C_QB + 2 * B_W])])
        for h in range(2):
            l0 = h * CMP_LEN // 2
            loads.append([(lambda i, a=a: slot(i, k=16)[a * HD:(a + 1) * HD, :, :],
                           w.rearrange("o (l d) n -> d (o l) n", d=HD)[:, l0:l0 + 16, :])
                          for a, w in enumerate((cmp_w1_k, cmp_w1_v))])
        for s in (4, 3, 2, 5):
            for h in range(2):
                loads.append([(slot, wada[:, :, s * D + h * BANK:s * D + (h + 1) * BANK])])
        L_SC, L_TOK, L_QKB, L_W1, L_ADA2, L_MIX = 0, 4, 8, 9, 11, 19

        def slot_of(i):
            return i % 3 if i < L_MIX else (i - L_MIX) % 2

        slot_n = [[] for _ in range(3)]
        w_count = []
        for i, parts in enumerate(loads):
            s = slot_of(i)
            w_count.append(16 * len(parts) + (w_count[slot_n[s][-1]] if slot_n[s] else 0))
            slot_n[s].append(i)

        def prev_of(i):
            s = slot_n[slot_of(i)]
            return s[s.index(i) - 1] if s.index(i) else None

        def wait_load(eng, i):
            eng.wait_ge(w_in_slot[slot_of(i)], w_count[i])

        def wait_used(eng, i):
            if i < L_TOK:
                eng.wait_ge(w_used, i + 1)
            elif i <= L_QKB:
                eng.wait_ge(acc_full, NT * (i - L_TOK + 1))
            elif i < L_ADA2:
                eng.wait_ge(hid_full, 1)
            elif i < L_MIX:
                eng.wait_ge(w_used, 4 + i - L_ADA2 + 1)
            elif i < L_MIX + NK:
                eng.wait_ge(mix_full, mixed_count(6 * (i - L_MIX + 1) - 1))
            else:
                eng.wait_ge(out_full, NT)

        prob = [tmp[:, i * T:(i + 1) * T] for i in range(2)]
        probT = [tmp[:, (2 + i) * T:(3 + i) * T] for i in range(2)]
        att = arena[:, SLOT:3 * SLOT]
        zs, zc, zl, cum, prob_b = (att[:, i * T:(i + 1) * T] for i in range(5))
        cmp_s, cmp_p = att[:, 5120:5632], att[:, 5632:6144]
        swa_s = [att[:, 6144 + i * 256:6400 + i * 256] for i in range(2)]
        part, o_tok = att[:, 6656:7168], att[:, 7168:8192]
        negm = sb("negm", [P, 4])
        cmp_m, cmp_r = sb("cmp_m", [P, NSA_H]), sb("cmp_r", [P, NSA_H])
        imp = sb("imp", [P, NC + 2])
        imp_b, top, sel = sb("imp_b", [P, 2, NSEL]), sb("top", [P, 8]), sb("sel", [P, AUG])
        den = sb("den", [P, 2, 2 * NSA_H + SWA_H])
        sink, sink_e, coef = sb("sink", [P, SWA_H]), sb("sink_e", [P, SWA_H]), sb("coef", [P, 2 * NSA_H + SWA_H])

        units, slots = [], []
        for n in range(NT):
            lo = max(0, n - NSA_WINDOW // P)
            order = [("win", h, lo) for h in range(NSA_H)]
            for h in range(NSA_H):
                order.append(("slc", h, 0))
                if h % 2 == 0:
                    order.append(("swa", h // 2, max(0, n - 1)))
            for i, (kind, h, lo) in enumerate(order):
                slots.append(dict(n=n, i=i, unit=dict(kind=kind, h=h, n=n, lo=lo), ride=None, extra=[]))
            for h, i in enumerate((6, 9, 12, 15)):
                slots[-len(order) + i]["ride"] = dict(kind="sb", h=h, n=n, lo=0)
        per_tile = len(order)
        for i in range(6):
            slots.append(dict(n=NT, i=i, unit=None, ride=None, extra=[]))
        n_s, n_g, n_v = 0, 0, 0
        before = None
        for q, s in enumerate(slots):
            s["S"] = []
            if s["i"] == 0 and s["n"] < NT:
                s["S"].append(dict(kind="cmp", n=s["n"], h=0))
                s["cmp"] = s["S"][0]
            if s["unit"]:
                s["unit"]["slot"] = q
                s["S"].append(s["unit"])
            if s["ride"]:
                s["S"].append(s["ride"])
            for u in s["S"]:
                u["s"] = n_s
                n_s += 1
            s["T"] = []
            if q and slots[q - 1]["unit"]:
                s["T"].append(slots[q - 1]["unit"])
            if q >= 4 and slots[q - 4]["ride"]:
                s["T"].append(slots[q - 4]["ride"])
            tile0 = q - s["i"]
            if s["i"] == 3 and s["n"] < NT:
                s["T"].append(slots[tile0]["cmp"])
            if s["i"] == 5 and s["n"] < NT:
                s["T"].append(dict(kind="sel", n=s["n"], h=0))
                s_sel = s["T"][-1]
                for k in range(per_tile):
                    if slots[tile0 + k]["unit"]["kind"] == "slc":
                        slots[tile0 + k]["unit"]["sel"] = s_sel
            if s["i"] == 4 and s["n"]:
                s["T"].append(dict(kind="out", n=s["n"] - 1, h=0))
            for u in s["T"]:
                u["nb"] = {"cmp": 4, "sel": 1, "out": 8}.get(u["kind"]) or u["n"] + 1 - u["lo"]
                u["groups"] = list(range(n_g, n_g + -(-u["nb"] // 4)))
                n_g += len(u["groups"])
                if u["kind"] not in ("sel", "out"):
                    u["v"] = n_v
                    n_v += 1
        by_v = {u["v"]: u for s in slots for u in s["T"] if "v" in u}
        last_v = {}
        for v, u in by_v.items():
            last_v[(u["kind"], u["n"])] = v
        by_s = [u for s in slots for u in s["S"]]
        sel_of = {u["n"]: u for s in slots for u in s["T"] if u["kind"] == "sel"}
        out_of = {u["n"]: u for s in slots for u in s["T"] if u["kind"] == "out"}
        rides = [s["ride"] for s in slots if s["ride"]]
        t_free = [sem("t_free0"), sem("t_free1")]
        t_full, s_full, pv_done, max_ok, p_ok, pb_ok = (sem(s) for s in (
            "t_full", "s_full", "pv_done", "max_ok", "p_ok", "pb_ok"))
        cmp_in, cmp_e, cmp_pok, sel_ok, o_read, o_ok = (sem(s) for s in (
            "cmp_in", "cmp_e", "cmp_pok", "sel_ok", "o_read", "o_ok"))
        sb_z, sb_zc, sb_ln, sb_sp, sb_arg, sink_in = (sem(s) for s in (
            "sb_z", "sb_zc", "sb_ln", "sb_sp", "sb_arg", "sink_in"))

        def ride(q, d):
            r = slots[q - d]["ride"] if q >= d else None
            return (r, width(r), r["n"] * SB_H + r["h"]) if r else (None, 0, 0)

        def score_buf(u):
            return psum[:, 2 * (u["s"] % 2):2 * (u["s"] % 2) + 2, :].rearrange("p a b -> p (a b)")

        def wait_evacuated(eng, g):
            eng.wait_ge(t_free[g % 2], g // 2 + 1)

        def wait_scores_read(eng, i):
            u = by_s[i]
            if u["kind"] == "cmp":
                eng.wait_ge(cmp_in, u["n"] + 1)
            elif u["kind"] == "sb":
                eng.wait_ge(sb_z, u["n"] * SB_H + u["h"] + 1)
            elif u["kind"] == "swa":
                eng.wait_ge(max_ok, u["slot"] + 1)
            else:
                eng.wait_ge(p_ok, u["slot"] + 1)

        def width(u):
            return (u["n"] + 1 - u["lo"]) * P

        def group(u, j):
            return psum[:, 4 + u["groups"][j] % 2, :], range(4 * j, min(4 * j + 4, u["nb"]))

        def evacuate_groups(eng, u, parity):
            for j, g in enumerate(u["groups"]):
                if g % 2 != parity:
                    continue
                bank, blocks = group(u, j)
                w = len(blocks) * P
                eng.wait_ge(t_full, g + 1)
                if u["kind"] == "sel":
                    src = bank[ROW_SEL:AUG, 0:P].unsqueeze(1).to_broadcast([NSEL, NSA_H, P])
                    dst = qaT[ROW_SEL:AUG, u["n"], :, :]
                elif u["kind"] == "out":
                    src, dst = bank, heads[:, (u["n"] * 2 + j) * BANK:(u["n"] * 2 + j + 1) * BANK]
                else:
                    if u["v"] >= 2:
                        eng.wait_ge(pv_done, u["v"] - 1)
                    src, dst = bank[:, 0:w], probT[u["v"] % 2][:, 4 * j * P:4 * j * P + w]
                if parity == 0:
                    ins = nc.scalar.activation(dst, src, ACT.Copy)
                else:
                    ins = nc.vector.tensor_copy(dst, src)
                ins.then_inc(t_free[parity], 1)

        for m in range(NK):
            loads.append([(lambda i, b=b: mix_gate(i)[:, b, :, :],
                           win[:, :, C_MERGE + b * D + m * P:C_MERGE + b * D + (m + 1) * P]) for b in range(3)] +
                         [(lambda i, k0=k0, k1=k1: mix_branch(i)[:, k0:k1, :],
                           w.rearrange("l (k p) n -> p (l k) n", p=P)[:, :, m * P:(m + 1) * P])
                          for w, k0, k1 in ((w_branch_a, 0, 4), (w_branch_b, 4, 6), (w_branch_c, 6, 8))])
        for h in range(2):
            loads.append([(slot, w_out.rearrange("l (k p) n -> p (l k) n", p=P)[:, :, h * BANK:(h + 1) * BANK])])
        L_OUT = L_MIX + NK
        for i in range(L_MIX, len(loads)):
            s = slot_of(i)
            w_count.append(16 * len(loads[i]) + w_count[slot_n[s][-1]])
            slot_n[s].append(i)

        def mixed_count(r):
            return 2 * (r + 1)

        def mix_gate(i):
            return arena[:, i * SLOT:i * SLOT + 3 * NK * P].rearrange("p (b k n) -> p b k n", b=3, k=NK)

        def mix_branch(i):
            return arena[:, i * SLOT + 3 * NK * P:(i + 1) * SLOT].rearrange("p (k n) -> p k n", k=NK)

        h_hi, h_lo = (arena_r[:, 2 * i * SLOT:2 * (i + 1) * SLOT].rearrange("p (k t) -> p k t", k=NK) for i in (1, 2))
        h_split, h_rest, w_split, w_rest = sem("h_split"), sem("h_rest"), sem("w_split"), sem("w_rest")

        def gate_hi(t):
            return kv_r[:, 2 * D + t % 4 * NK * P:2 * D + (t % 4 + 1) * NK * P].rearrange("p (k n) -> p k n", k=NK)

        def gate_lo(t):
            a = slot_of(L_MIX + t // 3) * SLOT + t % 3 * NK * P
            return arena_r[:, a:a + NK * P].rearrange("p (k n) -> p k n", k=NK)

        def gate_raw(t):
            return mix_gate(slot_of(L_MIX + t // 3))[:, t % 3, :, :]

        def tokens_hi(act, hf):
            ts = slice(hf * BANK, (hf + 1) * BANK)
            act.activation(h_hi[:, :, ts], hT[:, :, ts], ACT.Copy).then_inc(h_split, 1)

        def tokens_lo(dve, hf):
            ts = slice(hf * BANK, (hf + 1) * BANK)
            dve.wait_ge(h_split, hf + 1)
            dve.tensor_tensor(h_lo[:, :, ts], hT[:, :, ts], h_hi[:, :, ts].bitcast(F32), ALU.subtract).then_inc(h_rest, 1)

        def weights_hi(act, t):
            if t < 3 * NK:
                wait_load(act, L_MIX + t // 3)
                if t >= 4:
                    act.wait_ge(mix_full, mixed_count(2 * (t - 4) + 1))
                act.activation(gate_hi(t), gate_raw(t), ACT.Copy).then_inc(w_split, 1)

        def weights_lo(dve, t):
            if t < 3 * NK:
                dve.wait_ge(w_split, t + 1)
                dve.tensor_tensor(gate_lo(t), gate_raw(t), gate_hi(t).bitcast(F32),
                                  ALU.subtract).then_inc(w_rest, 1)

        oT = heads[:, :].rearrange("p (n k t) -> p n k t", n=NT, k=NK)
        yT = bc[:, :].rearrange("p (k t) -> p k t", k=NK)
        x1 = heads[:, :].rearrange("p (n d) -> p n d", n=NT)
        sig = [kv[:, i * BANK:(i + 1) * BANK] for i in range(2)]
        gated = kv[:, 2 * BANK:3 * BANK]
        xr = [kv[:, (2 + i) * D:(3 + i) * D] for i in range(2)]
        xn2, h2T = kv[:, 4 * D:5 * D], kv[:, 5 * D:6 * D].rearrange("p (k t) -> p k t", k=NK)
        wr, rbias = sb("wr", [P, NK, NE]), sb("rbias", [P, NE])
        N_BLK = 2 * T // P + NE
        xn_dram = nc.dram_tensor("xn_dram", [T, D], F32, kind="Internal").ap()
        y_dram = nc.dram_tensor("y_dram", [N_BLK * P, D], F32, kind="Internal").ap()
        slot_tok = nc.dram_tensor("slot_tok", [(N_BLK + 1) * P, 1], U32, kind="Internal").ap()
        mix_full, sig_ok, mix_done, y_ok = (sem(s) for s in ("mix_full", "sig_ok", "mix_done", "y_ok"))
        xr_in = [sem("xr_in0"), sem("xr_in1")]
        out_full, x1_ok, x1_sq, x1_rstd, xn2_ok, xn2_out, xn2T_full, h2T_act, h2T_dve, rt_full = (sem(s) for s in (
            "out_full", "x1_ok", "x1_sq", "x1_rstd", "xn2_ok", "xn2_out", "xn2T_full", "h2T_act", "h2T_dve", "rt_full"))
        wr_in = sem("wr_in")

        route = [kv[:, i * P:(i + 1) * P] for i in range(12)]
        r3 = [r.rearrange("p (n e) -> p n e", n=NT) for r in route]
        iota_e, iota_m = sb("iota_e", [P, NE]), sb("iota_m", [P, NT])
        chosen = sb("chosen", [P, P], BF16)
        ones_b, before_b = sb("ones_b", [P, P], BF16), sb("before_b", [P, P], BF16)
        w12, dest_f = sb("w12", [P, 2, NT]), sb("dest_f", [P, 2, NT])
        dest = sb("dest", [P, 2, NT], U32)
        plan_f, plan_i = sb("plan_f", [P, 2 * NE + 2]), sb("plan_i", [P, 2 * NE + 2], I32)
        tok_id, zero_u = sb("tok_id", [P, NT], U32), sb("zero_u", [P, N_BLK + 1], U32)
        score_ok, chosen_ok, rank_full, dest_ok, table_zero, table_ok, routing_tables = (sem(s) for s in (
            "score_ok", "chosen_ok", "rank_full", "dest_ok", "table_zero", "table_ok", "routing_tables"))

        xs, xsT = kv[:, 2 * D:3 * D], kv[:, 3 * D:4 * D].rearrange("p (k t) -> p k t", k=NK)
        silu_g, act_a = kv[:, 4 * D:4 * D + BANK], kv[:, 4 * D + BANK:5 * D]
        aT = bc[:, 0:BANK].rearrange("p (k t) -> p k t", k=4)
        y_sb = bc[:, D:2 * D]
        idx = sb("idx", [P, 1], U32)
        expert_w = [sem(f"expert_w{i}") for i in range(6)]
        idx_in, xs_in, xsT_half, xsT_full, xsT_act, xsT_dve = (sem(s) for s in ("idx_in", "xs_in", "xsT_half", "xsT_full", "xsT_act", "xsT_dve"))
        gate_full, up_full, silu_ok, a_ok, aT_full, aT_ok, y_full, y_act, y_dve, y_out = (
            sem(s) for s in ("gate_full", "up_full", "silu_ok", "a_ok", "aT_full", "aT_ok", "y_full", "y_act", "y_dve",
                             "y_out"))
        wge, wue, wde = (w.rearrange("l e (k p) n -> (l e) p k n", p=P) for w in (w_exp_gate, w_exp_up, w_exp_down))

        pair = [[arena[:, (2 * n + j) * D:(2 * n + j + 1) * D] for j in range(2)] for n in range(NT)]
        res = [arena[:, (2 * NT + n) * D:(2 * NT + n + 1) * D] for n in range(NT)]
        pair_in = [sem(f"pair_in{n}") for n in range(NT)]
        scaled, comb_ok, out_st = sem("scaled"), sem("comb_ok"), sem("out_st")
        spare_out = sem("spare_out")
        pool_go, sp_go = sem("pool_go"), sem("sp_go")

        block = ctx.enter_context(nc.Block())

        @block.sync
        def _(sp):
            def load(i):
                p = prev_of(i)
                if p is not None:
                    wait_used(sp, p)
                for place, src in loads[i]:
                    sp.dma_start(place(slot_of(i)), src).then_inc(w_in_slot[slot_of(i)], 16)

            for r, (src, n) in enumerate(((c, NK), (g_norm_mix, NK), (g_norm_moe, NK))):
                sp.dma_start(rows[r * NK:(r + 1) * NK, :], src.rearrange("o (k p) -> (o k) p", p=P)).then_inc(small_in, 16)
            sp.dma_start(rows[3 * NK:9 * NK, :], b_ada.rearrange("o (k p) -> (o k) p", p=P)).then_inc(small_in, 16)
            for a, g in enumerate((cmp_pe_k, cmp_pe_v)):
                sp.dma_start(pe_rows[:, a * HD:(a + 1) * HD], g.rearrange("o l d -> (o l) d")).then_inc(small_in, 16)
            for n in range(3):
                sp.dma_start(xt[n], x2d[n * P:(n + 1) * P, :]).then_inc(x_in[n % 3], 16)
                load(n)
            load(3)
            load(4)
            for n in range(3, NT):
                sp.wait_ge(xT_full, n - 2)
                sp.dma_start(xt[n % 3], x2d[n * P:(n + 1) * P, :]).then_inc(x_in[n % 3], 16)
                if n < 5:
                    load(n + 2)
            for i in range(7, L_MIX):
                load(i)
            load(L_MIX)
            sp.dma_start(wr[:, :, :], w_router.rearrange("(k p) e -> p k e", p=P)).then_inc(wr_in, 16)
            sp.dma_start(rbias[:, :], router_bias.partition_broadcast(P)).then_inc(wr_in, 16)
            sp.wait_ge(t_full, n_g)
            for i in range(L_MIX + 1, len(loads)):
                load(i)
            def load_expert(e, q, which=(0, 1, 2)):
                for j in which:
                    w = (wge, wue, wde)[j]
                    sp.dma_start(slot(3 * q + j, k=w.shape[2]), w[e]).then_inc(expert_w[3 * q + j], 16)

            wait_used(sp, L_OUT - 1)
            load_expert(1, 1)
            load_expert(0, 0, (2,))
            sp.wait_ge(mix_done, 3 * 2 * NK)
            for n in range(NT):
                if n >= 2:
                    sp.wait_ge(xn2_ok, n - 1)
                sp.dma_start(xr[n % 2], x2d[n * P:(n + 1) * P, :]).then_inc(xr_in[n % 2], 16)
                if n:
                    sp.wait_ge(xn2_ok, n)
                    sp.dma_start(xn_dram[(n - 1) * P:n * P, :], xn2).then_inc(xn2_out, 16)
            sp.wait_ge(xn2_ok, NT)
            sp.dma_start(xn_dram[(NT - 1) * P:NT * P, :], xn2).then_inc(xn2_out, 16)

            wait_used(sp, L_OUT + 1)
            load_expert(0, 0, (0, 1))
            sp.wait_ge(dest_ok, 1)

            def next_experts(e2):
                for q in range(2):
                    at = e2 * 2 + (NE + q - 1)
                    b_next = sp.value_load(plan_i[0:1, bass.ds(at, 1)], min_val=1, max_val=N_BLK - 1)
                    sp.wait_ge(y_full, b_next)
                    sp.nop().then_inc(sp_go, 1)
                    load_expert(e2 * 2 + q if isinstance(e2, int) else sp.snap(e2 * 2 + q), q)

            next_experts(1)
            n_spare = sp.value_load(plan_i[0:1, 2 * NE + 1:2 * NE + 2], min_val=1, max_val=N_BLK - NE)
            with sp.Fori(0, n_spare) as j:
                sp.dma_start(y_dram[bass.ds((N_BLK - 1) * P - j * P, P), :], x2d[0:P, :]).then_inc(spare_out, 16)
            with sp.Fori(2, NE // 2) as e2:
                next_experts(e2)
            for n in range(NT):
                sp.wait_ge(comb_ok, n + 1)
                sp.dma_start(out2d[n * P:(n + 1) * P, :], res[n]).then_inc(out_st, 16)
            sp.wait_ge(out_st, 16 * NT)

        @block.gpsimd
        def _(pool):
            one = Chain(pool, pool_own)
            one(pool.memset(ident[:, :], 0.0))
            one(pool.affine_select(out=ident[:, :], in_=ident[:, :], compare_op=ALU.not_equal, fill=1.0, base=0,
                                   pattern=[[-1, P]], channel_multiplier=1))
            one(pool.tensor_copy(identb[:, :], ident[:, :]))
            one(pool.memset(gain[ROW_POS:ROW_SEL, 0:1], 8.0))
            pool.memset(half[:, :], -0.5).then_inc(tables, 1)
            for i, g in enumerate((nsa_q_gain, nsa_k_gain[:, 0, :], nsa_k_gain[:, 1, :], nsa_k_gain[:, 2, :],
                                   swa_q_gain, swa_k_gain)):
                for lo in ((0,) if i < 4 else (0, HD)):
                    pool.dma_start(gain[lo:lo + HD, i:i + 1], g.rearrange("o d -> d o")).then_inc(gain_in, 16)
            for a, g in enumerate((cmp_w2_k, cmp_w2_v)):
                pool.dma_start(w2[:, a, :, :], g.rearrange("o (c p) d -> p (o c) d", p=P)).then_inc(gain_in, 16)
            pool.dma_start(ga_bc[:, :], b_ada[0, 2 * D:3 * D].partition_broadcast(P)).then_inc(gain_in, 16)
            pool.dma_start(gm_bias, b_ada[0, 5 * D:6 * D].partition_broadcast(P)).then_inc(gain_in, 16)



            for n in range(NT):
                pool.wait_ge(x_sq, n + 1)
                m = stp[:, n:n + 1]
                one(pool.tensor_scalar(m, st[:, SSX + n:SSX + n + 1], 1.0 / D, EPS, ALU.mult, ALU.add))
                pool.tensor_tensor(m, m, half[:, 0:1], ALU.pow).then_inc(x_rstd, 1)
            pool.wait_ge(x_rstd, NT)
            pool.memset(heads[ROW_POS:ROW_SEL, :], 0.0).then_inc(tables, 1)
            pool.wait_ge(tables, 2)
            for s in range(4 * NT):
                ng = (NSA_H, 2, SWA_H, 2)[s // NT]
                m, r = stp[:, 8:8 + ng], stp[:, 16:16 + ng]
                pool.wait_ge(reduced, s + 1)
                if s:
                    pool.wait_ge(tok_ok, s)
                one(pool.tensor_scalar(m, st[:, SQ:SQ + ng], 1.0 / HD, EPS, ALU.mult, ALU.add))
                pool.tensor_tensor(r, m, half[:, 0:ng], ALU.pow).then_inc(rstd_ok, 1)
            pool.wait_ge(rstd_ok, 4 * NT)
            for t, base, step, mult in ((tri_causal, 0, -1, 1), (tri_low, -1, 1, -1), (tri_strict, -1, -1, 1)):
                one(pool.memset(t[:, :], 0.0))
                one(pool.affine_select(out=t[:, :], in_=t[:, :], compare_op=ALU.is_ge, fill=MASKED, base=base,
                                       pattern=[[step, P]], channel_multiplier=mult))
            one(pool.memset(stair[:, :], 0.0))
            one(pool.affine_select(out=stair[:, :], in_=stair[:, :], compare_op=ALU.is_ge, fill=MASKED,
                                   base=16 * 56 - (CMP_LEN - 1), pattern=[[-CMP_STRIDE, 120]], channel_multiplier=1))
            one(pool.iota(swa_bias[:, 0, :], pattern=[[-1, 2 * P]], base=P, channel_multiplier=1,
                          allow_small_or_imprecise_dtypes=True))
            for h in reversed(range(SWA_H)):
                one(pool.tensor_scalar(swa_bias[:, h, :], swa_bias[:, 0, :], -alibi_slope(h), 0.0, ALU.mult, ALU.add))
            for h in range(SWA_H):
                one(pool.affine_select(out=swa_bias[:, h, :], in_=swa_bias[:, h, :], compare_op=ALU.is_ge,
                                       fill=MASKED, base=P, pattern=[[-1, 2 * P]], channel_multiplier=1))
                one(pool.affine_select(out=swa_bias[:, h, :], in_=swa_bias[:, h, :], compare_op=ALU.is_ge,
                                       fill=MASKED, base=-1, pattern=[[1, 2 * P]], channel_multiplier=-1))
            for k in (kwinT, kslcT):
                pos = k[ROW_POS:ROW_SEL, :]
                one(pool.iota(pos, pattern=[[1, T]], base=0, channel_multiplier=0, allow_small_or_imprecise_dtypes=True))
                one(pool.affine_select(out=pos, in_=pos, compare_op=ALU.is_equal, fill=0.0, base=0,
                                       pattern=[[0, T]], channel_multiplier=1))
            blocks = kslcT[ROW_SEL:AUG, :]
            one(pool.memset(blocks, 1.0))
            one(pool.affine_select(out=blocks, in_=blocks, compare_op=ALU.is_ge, fill=0.0, base=0,
                                   pattern=[[1, T]], channel_multiplier=-SEL_BLOCK))
            one(pool.affine_select(out=blocks, in_=blocks, compare_op=ALU.is_ge, fill=0.0, base=SEL_BLOCK - 1,
                                   pattern=[[-1, T]], channel_multiplier=SEL_BLOCK))
            cend = kcmpT[ROW_POS:ROW_SEL, :]
            one(pool.iota(cend, pattern=[[CMP_STRIDE, NC + 1]], base=CMP_LEN - 1, channel_multiplier=0,
                          allow_small_or_imprecise_dtypes=True))
            one(pool.affine_select(out=cend, in_=cend, compare_op=ALU.is_equal, fill=0.0, base=0,
                                   pattern=[[0, NC + 1]], channel_multiplier=1))
            one(pool.iota(force[:, :, :], pattern=[[-2, NT], [1, NSEL]], base=0, channel_multiplier=0,
                          allow_small_or_imprecise_dtypes=True))
            pool.iota(stp[:, 30:31], pattern=[[0, 1]], base=0, channel_multiplier=1,
                      allow_small_or_imprecise_dtypes=True).then_inc(tables, 1)

            pool.wait_ge(tables, 3)
            pool.wait_ge(kcmp_sq, 1)
            one(pool.tensor_scalar(stp[0:HD, 8:9], st[0:HD, SQ:SQ + 1], 1.0 / HD, EPS, ALU.mult, ALU.add))
            pool.tensor_tensor(stp[0:HD, 16:17], stp[0:HD, 8:9], half[0:HD, 0:1], ALU.pow).then_inc(kcmp_rstd, 1)
            pool.dma_start(sink[:, :], swa_sinks[0, :].partition_broadcast(P)).then_inc(sink_in, 16)
            pool.wait_ge(mod2_ok, 1)
            for m, r in enumerate(rides):
                w = width(r)
                pool.wait_ge(sb_z, m + 1)
                if m:
                    pool.wait_ge(sb_arg, m)
                pool.tensor_scalar(zl[:, 0:w], zs[:, 0:w], 40.0, 0.0, ALU.subtract, ALU.max).then_inc(sb_sp, 1)
            one(pool.iota(iota_e[:, :], pattern=[[1, NE]], base=0, channel_multiplier=0,
                          allow_small_or_imprecise_dtypes=True))
            one(pool.iota(iota_m[:, :], pattern=[[P, NT]], base=0, channel_multiplier=0,
                          allow_small_or_imprecise_dtypes=True))
            one(pool.iota(tok_id[:, :], pattern=[[P, NT]], base=0, channel_multiplier=1))
            one(pool.memset(zero_u[:, :], 0))
            one(pool.memset(ones_b[:, :], 1.0))
            one(pool.memset(before_b[:, :], 1.0))
            pool.affine_select(out=before_b[:, :], in_=before_b[:, :], compare_op=ALU.is_gt, fill=0.0, base=0,
                               pattern=[[1, P]], channel_multiplier=-1).then_inc(routing_tables, 1)
            pool.dma_start(slot_tok.rearrange("(p j) o -> p (j o)", p=P), zero_u[:, :]).then_inc(table_zero, 16)
            for n in range(NT):
                pool.wait_ge(x1_sq, n + 1)
                one(pool.tensor_scalar(stp[:, 0:1], st[:, SSX:SSX + 1], 1.0 / D, EPS, ALU.mult, ALU.add))
                pool.tensor_tensor(stp[:, 1:2], stp[:, 0:1], half[:, 0:1], ALU.pow).then_inc(x1_rstd, 1)
            pool.wait_ge(table_zero, 16)
            pool.wait_ge(dest_ok, 1)
            for n in range(NT):
                for j in range(2):
                    pool.indirect_dma_start(slot_tok, bass.IndirectOffsetOnAxis(ap=dest[:, j, n:n + 1], axis=0),
                                            tok_id[:, n:n + 1], None).then_inc(table_ok, 16)
            pool.wait_ge(table_ok, 16 * 2 * NT)
            pool.wait_ge(xn2_out, 16 * NT)
            n_blk = pool.value_load(plan_i[0:1, 2 * NE:2 * NE + 1], min_val=NE, max_val=N_BLK - 1)
            def load_list(j):
                pool.dma_start(idx[:, :], slot_tok[bass.ds(j * P, P), :] if not isinstance(j, int) else slot_tok[0:P, :]).then_inc(idx_in, 16)

            load_list(0)
            with pool.Fori(0, n_blk + 1) as j:
                pool.wait_ge(idx_in, j * 16 + 16)
                pool.wait_ge(xsT_full, j + 1)
                pool.nop().then_inc(pool_go, 1)
                pool.indirect_dma_start(xs, None, xn_dram, bass.IndirectOffsetOnAxis(ap=idx[:, 0:1], axis=0)
                                        ).then_inc(xs_in, 16)
                pool.wait_ge(xs_in, j * 16 + 16)
                load_list(j + 1)
            n_spare = pool.value_load(plan_i[0:1, 2 * NE + 1:2 * NE + 2], min_val=1, max_val=N_BLK - NE)
            pool.wait_ge(y_out, n_blk * 16 + 16)
            pool.wait_ge(spare_out, n_spare * 16)
            pool.nop().then_inc(pool_go, 1)
            for n in range(NT):
                for j in range(2):
                    pool.indirect_dma_start(pair[n][j], None, y_dram,
                                            bass.IndirectOffsetOnAxis(ap=dest[:, j, n:n + 1], axis=0)
                                            ).then_inc(pair_in[n], 16)

        @block.scalar
        def _(act):
            own = Chain(act, act_own)
            act.wait_ge(rowsT, 1)
            act.wait_ge(cond_ok, 1)
            act.activation(cond[:, :], cols[:, 0:NK], ACT.Exp, scale=-1.0).then_inc(cond_e, 1)
            for n in range(NT + 1):
                if n < NT:
                    act.wait_ge(x_in[n % 3], 16 * (n // 3 + 1))
                    if n:
                        act.wait_ge(x_sq, n)
                    act.activation(psum[:, 4:6, :], xt[n % 3].rearrange("p (a d) -> p a d", a=2), ACT.Square,
                                   accum_out=st[:, SSX + n:SSX + n + 1]).then_inc(x_sq, 1)
                if n:
                    m = n - 1
                    act.wait_ge(xT_full, m + 1)
                    act.wait_ge(mod_ok, 1)
                    for k in range(4, 8):
                        ins = act.activation(hT[:, k, m * P:(m + 1) * P],
                                             psum[:, 2 * (m % 2) + 1, (k - 4) * P:(k - 3) * P], ACT.Identity,
                                             bias=mod_b[:, k:k + 1], scale=mod_a[:, k:k + 1])
                    ins.then_inc(hT_act, 1)
            act.wait_ge(gain_in, 16 * 12)
            act.wait_ge(tables, 2)
            for s in range(4 * NT + 1):
                ch, n = divmod(s, NT)
                a = psum[:, 4 + s % 3, :]
                if s < 4 * NT:
                    act.wait_ge(acc_full, s + 1)
                    if s:
                        act.wait_ge(reduced, s)
                    if ch == 0:
                        act.activation(sq[:, 0:A_W], a[:, 0:A_W], ACT.Square).then_inc(squared, 1)
                    elif ch == 1:
                        k2 = a[:, 2 * HD:6 * HD].rearrange("p (g a d) -> p g a d", g=2, a=2)[:, :, 0, :]
                        act.activation(v_slc[:, n, :], a[:, 3 * HD:4 * HD], ACT.Copy)
                        act.activation(v_win[:, n, :], a[:, 5 * HD:6 * HD], ACT.Copy)
                        act.activation(gates[:, n, :], a[:, 6 * HD:6 * HD + 3 * NSA_H], ACT.Sigmoid)
                        act.activation(sq[:, 0:2 * HD].rearrange("p (g d) -> p g d", g=2), k2,
                                       ACT.Square).then_inc(squared, 1)
                    elif ch == 2:
                        act.activation(v_b[:, n, :], a[:, 0:B_W], ACT.Copy)
                        act.activation(sq[:, 0:C_W], a[:, B_W:B_W + C_W], ACT.Square).then_inc(squared, 1)
                    else:
                        act.activation(v_c[:, n, :], a[:, 2 * HD:4 * HD], ACT.Copy)
                        act.activation(sq[:, 0:2 * HD], a[:, 0:2 * HD], ACT.Square).then_inc(squared, 1)
                if s:
                    r = s - 1
                    pch, m = divmod(r, NT)
                    ts = slice(m * P, (m + 1) * P)
                    b0, b1 = psum[:, 2 * (r % 2), :], psum[:, 2 * (r % 2) + 1, :]
                    act.wait_ge(tokT_full, r + 1)
                    if pch == 0:
                        ins = act.activation(qaT[0:ROW_POS + 1, m, 4:8, :], b1[0:ROW_POS + 1, :].rearrange("p (h t) -> p h t", h=4),
                                             ACT.Copy, scale=gain_q8[0:ROW_POS + 1, :])
                    elif pch == 1:
                        act.activation(kslcT[0:HD, ts], b1[0:HD, 0:P], ACT.Copy, scale=G_KS[0:HD, :])
                        ins = act.activation(kwinT[0:HD, ts], b1[0:HD, P:2 * P], ACT.Copy, scale=G_KW[0:HD, :])
                    elif pch == 2:
                        ins = act.activation(qcT[:, 1, ts], b1[:, 0:P], ACT.Copy, scale=gain_sq8[:, :])
                    else:
                        ins = act.activation(kcT[:, 1, ts], b1[:, 0:P], ACT.Copy, scale=G_SK)
                    ins.then_inc(tokT_act, 1)
            for s in range(4 * NT, 4 * NT + 8, 2):
                cc = (s - 4 * NT) // 2
                act.wait_ge(acc_full, s + 1)
                act.activation((qbT if cc < 2 else kbT)[:, cc % 2, 0:BANK], psum[:, 4 + s % 3, :], ACT.Copy,
                               scale=HD ** -0.5 if cc < 2 else 1.0).then_inc(acc_act, 1)
            act.wait_ge(gelu_in, 1)
            ge = tmp_ge
            act.activation(ge, ge, ACT.Exp, scale=-GELU_C).then_inc(gelu_e, 1)
            act.wait_ge(kcmp_full, 1)
            act.activation(sq[0:HD, 0:HD], psum[0:HD, 2, 0:HD], ACT.Square,
                           accum_out=st[0:HD, SQ:SQ + 1]).then_inc(kcmp_sq, 1)
            act.wait_ge(mod2_ok, 1)
            act.wait_ge(sink_in, 16)
            act.preload_act_table_set("natural_log_exp_and_others")
            for q, s in enumerate(slots):
                u = s["unit"]
                if u:
                    k, w = u["kind"], width(u)
                    act.wait_ge(max_ok, q + 1)
                    if q >= 2:
                        act.wait_ge(t_full, slots[q - 2]["unit"]["groups"][-1] + 1)
                    src = score_buf(u)[:, 0:w]
                    col = {"win": 0, "slc": NSA_H, "swa": 2 * NSA_H}[k] + u["h"]
                    if k == "swa":
                        src = swa_s[u["h"] % 2][:, 0:w]
                        act.activation(sink_e[:, u["h"]:u["h"] + 1], sink[:, u["h"]:u["h"] + 1], ACT.Exp,
                                       bias=negm[:, q % 4:q % 4 + 1])
                    act.activation(prob[q % 2][:, 0:w], src, ACT.Exp, bias=negm[:, q % 4:q % 4 + 1],
                                   accum_out=den[:, u["n"] % 2, col:col + 1]).then_inc(p_ok, 1)
                for t in s["T"]:
                    evacuate_groups(act, t, 0)
                if "cmp" in s:
                    act.wait_ge(cmp_in, s["n"] + 1)
                    act.activation(cmp_p, cmp_s, ACT.Exp).then_inc(cmp_e, 1)
                r, w, m = ride(q, 1)
                if r:
                    act.wait_ge(sb_zc, m + 1)
                    own(act.activation(zc[:, 0:w], zc[:, 0:w], ACT.Exp))
                    act.activation(zc[:, 0:w], zc[:, 0:w], ACT.Ln, bias=1.0).then_inc(sb_ln, 1)
                r, w, m = ride(q, 3)
                if r:
                    act.wait_ge(sb_arg, m + 1)
                    if m:
                        act.wait_ge(t_full, rides[m - 1]["groups"][-1] + 1)
                    act.activation(prob_b[:, 0:w], zs[:, 0:w], ACT.Exp).then_inc(pb_ok, 1)
                r, w, m = ride(q, 0)
                if r:
                    act.wait_ge(s_full, r["s"] + 1)
                    if m:
                        act.wait_ge(pb_ok, m)
                    act.activation(zs[:, 0:w], score_buf(r)[:, 0:w], ACT.Copy).then_inc(sb_z, 1)
            act.wait_ge(t_full, n_g)
            act.wait_ge(pv_done, n_v)
            tokens_hi(act, 0)
            weights_hi(act, 0)
            tokens_hi(act, 1)
            weights_hi(act, 1)
            for r in range(3 * 2 * NK):
                if r % 2 == 0:
                    weights_hi(act, r // 2 + 2)
                act.wait_ge(mix_full, 2 * r + 1)
                if r >= 2:
                    act.wait_ge(mix_done, r - 1)
                act.activation(sig[r % 2], psum[:, 2 * (r % 4), :], ACT.Sigmoid).then_inc(sig_ok, 1)
            act.wait_ge(mix_done, 3 * 2 * NK)
            for n in range(NT + 1):
                if n < NT:
                    act.wait_ge(x1_ok, n + 1)
                    if n:
                        act.wait_ge(x1_rstd, n)
                    act.activation(xr[n % 2], x1[:, n, :], ACT.Square, accum_out=st[:, SSX:SSX + 1]).then_inc(x1_sq, 1)
                if n:
                    act.wait_ge(xn2T_full, n)
                    for k in range(4, 8):
                        ins = act.activation(h2T[:, k, :], psum[:, 5, (k - 4) * P:(k - 3) * P], ACT.Identity,
                                             bias=mod_b2[:, k:k + 1], scale=mod_a2[:, k:k + 1])
                    ins.then_inc(h2T_act, 1)
            act.wait_ge(rt_full, NT)
            act.activation(route[0], psum[:, 6, 0:P], ACT.Sigmoid).then_inc(score_ok, 1)
            def expert_tokens_act(j):
                act.wait_ge(xsT_full, j + 1)
                for k in range(4, 8):
                    ins = act.activation(xsT[:, k, :], psum[:, 3, (k - 4) * P:(k - 3) * P], ACT.Identity,
                                         bias=mod_b2[:, k:k + 1], scale=mod_a2[:, k:k + 1])
                ins.then_inc(xsT_act, 1)

            expert_tokens_act(1)
            act.wait_ge(dest_ok, 1)
            n_blk = act.value_load(plan_i[0:1, 2 * NE:2 * NE + 1], min_val=NE, max_val=N_BLK - 1)
            act.nop().then_inc(y_out, 16)
            act.nop().then_inc(y_act, 1)
            with act.Fori(0, n_blk) as j:
                act.wait_ge(gate_full, j + 1)
                act.activation(silu_g, psum[:, 0, :], ACT.Silu).then_inc(silu_ok, 1)
                act.wait_ge(aT_full, j + 1)
                act.activation(aT, psum[:, 4, :].rearrange("p (k t) -> p k t", k=4), ACT.Copy).then_inc(aT_ok, 1)
                expert_tokens_act(j + 2)
                act.wait_ge(y_full, j + 1)
                act.wait_ge(y_out, j * 16 + 16)
                act.activation(y_sb[:, BANK:D], psum[:, 6, :], ACT.Copy).then_inc(y_act, 1)
                act.wait_ge(y_act, j + 2)
                act.wait_ge(y_dve, j + 2)
                act.dma_start(y_dram[bass.ds(j * P, P), :], y_sb).then_inc(y_out, 16)
            for n in range(NT):
                act.wait_ge(pair_in[n], 32)
                act.activation(pair[n][0], pair[n][0], ACT.Copy, scale=w12[:, 0, n:n + 1]).then_inc(scaled, 1)

        @block.vector
        def _(dve):
            own = Chain(dve, dve_own)
            dve.wait_ge(rowsT, 1)
            own(dve.tensor_copy(peT[:, :], psum[:, 7, P:P + CMP_LEN]))
            dve.tensor_copy(cols[:, :], psum[:, 7, 0:9 * NK]).then_inc(cond_ok, 1)
            dve.wait_ge(cond_e, 1)
            own(dve.tensor_scalar(cond[:, :], cond[:, :], 1.0, None, ALU.add))
            own(dve.reciprocal(cond[:, :], cond[:, :]))
            own(dve.tensor_tensor(cond[:, :], cond[:, :], cols[:, 0:NK], ALU.mult))
            dve.tensor_copy(cond_bc, cond[:, :].unsqueeze(2).to_broadcast([P, NK, P])).then_inc(cond_ok, 1)

            def scale_shift(a, b, sc, sh, b_sc, b_sh, g):
                own(dve.scalar_tensor_tensor(a, sc, 1.0, cols[:, (3 + b_sc) * NK:(4 + b_sc) * NK], ALU.add, ALU.add))
                own(dve.tensor_tensor(a, a, cols[:, g * NK:(g + 1) * NK], ALU.mult))
                return dve.tensor_tensor(b, sh, cols[:, (3 + b_sh) * NK:(4 + b_sh) * NK], ALU.add)

            def copy_rows(bank, row_buf, used, before):
                for r in range(4):
                    dve.wait_ge(w_used, used + r + 1)
                    if r >= 2:
                        dve.wait_ge(turned, before + r - 1)
                    dve.tensor_copy(row_buf(r), psum[0:1, bank + r % 2, :]).then_inc(row_ok, 1)
                dve.wait_ge(turned, before + 4)

            for n in range(NT + 1):
                if n == 1:
                    copy_rows(0, early_row, 0, 0)
                    scale_shift(mod_a, mod_b, psum[:, 7, 0:NK], psum[:, 7, NK:2 * NK], 1, 0, 1).then_inc(mod_ok, 1)
                    dve.wait_ge(mod_ok, 1)
                if n < NT:
                    dve.wait_ge(x_rstd, n + 1)
                    dve.tensor_scalar(xt[n % 3], xt[n % 3], stp[:, n:n + 1], None, ALU.mult).then_inc(x_norm, 1)
                if n:
                    m = n - 1
                    dve.wait_ge(xT_full, m + 1)
                    for k in range(4):
                        ins = dve.tensor_scalar(hT[:, k, m * P:(m + 1) * P], psum[:, 2 * (m % 2), k * P:(k + 1) * P],
                                                mod_a[:, k:k + 1], mod_b[:, k:k + 1], ALU.mult, ALU.add)
                    ins.then_inc(hT_dve, 1)
            dve.wait_ge(tables, 2)
            dve.wait_ge(hT_act, NT)
            dve.wait_ge(gain_in, 16 * 12)
            for i in range(2):
                q8 = tok[i][:, 0:NSA_H * (HD + 1)].rearrange("p (h a) -> p h a", h=NSA_H)
                for h in range(NSA_H):
                    own(dve.memset(q8[:, h, HD:HD + 1], alibi_slope(SWA_H + h)))
            own(dve.tensor_scalar(gain_q8[0:ROW_SEL, :], G_Q[0:ROW_SEL, :], HD ** -0.5, None, ALU.mult))
            own(dve.tensor_scalar(gain_sq8[:, :], G_SQ, HD ** -0.5, None, ALU.mult))

            def evacuate(r):
                pch, m = divmod(r, NT)
                ts = slice(m * P, (m + 1) * P)
                b0 = psum[:, 2 * (r % 2), :]
                dve.wait_ge(tokT_full, r + 1)
                if pch == 0:
                    ins = dve.tensor_scalar(qaT[0:ROW_POS + 1, m, 0:4, :], b0[0:ROW_POS + 1, :].rearrange("p (h t) -> p h t", h=4),
                                            gain_q8[0:ROW_POS + 1, :], None, ALU.mult)
                elif pch == 1:
                    ins = dve.tensor_copy(kvcT[:, ts], b0[:, 0:P])
                elif pch == 2:
                    ins = dve.tensor_scalar(qcT[:, 0, ts], b0[:, 0:P], gain_sq8[:, :], None, ALU.mult)
                else:
                    ins = dve.tensor_scalar(kcT[:, 0, ts], b0[:, 0:P], G_SK, None, ALU.mult)
                ins.then_inc(tokT_dve, 1)

            for s in range(4 * NT + 1):
                ch, n = divmod(s, NT)
                a = psum[:, 4 + s % 3, :]
                if s < 4 * NT:
                    ng = (NSA_H, 2, SWA_H, 2)[ch]
                    dve.wait_ge(squared, s + 1)
                    if s:
                        dve.wait_ge(rstd_ok, s)
                    dve.tensor_reduce(st[:, SQ:SQ + ng], sq[:, 0:ng * HD].rearrange("p (g d) -> p g d", d=HD),
                                      AX.X, ALU.add).then_inc(reduced, 1)
                if s:
                    evacuate(s - 1)
                if s < 4 * NT:
                    t = tok[s % 2]
                    if s >= 2:
                        dve.wait_ge(tokT_full, s - 1)
                    dve.wait_ge(rstd_ok, s + 1)
                    r = stp[:, 16:16 + ng].unsqueeze(2).to_broadcast([P, ng, HD])
                    if ch == 0:
                        ins = dve.tensor_tensor(t[:, 0:NSA_H * (HD + 1)].rearrange("p (h a) -> p h a", h=NSA_H)[:, :, 0:HD],
                                                a[:, 0:A_W].rearrange("p (h d) -> p h d", d=HD), r, ALU.mult)
                    elif ch == 1:
                        dve.tensor_copy(t[:, 0:P], a[:, 0:P])
                        ins = dve.tensor_tensor(t[:, P:2 * P].rearrange("p (g d) -> p g d", g=2),
                                                a[:, 2 * HD:6 * HD].rearrange("p (g a d) -> p g a d", g=2, a=2)[:, :, 0, :],
                                                r, ALU.mult)
                    elif ch == 2:
                        ins = dve.tensor_tensor(t[:, 0:C_W].rearrange("p (h d) -> p h d", d=HD),
                                                a[:, B_W:B_W + C_W].rearrange("p (h d) -> p h d", d=HD), r, ALU.mult)
                    else:
                        t4 = t[:, 0:4 * HD].rearrange("p (g c d) -> p g c d", g=2, c=2)
                        for c2 in range(2):
                            ins = dve.tensor_tensor(t4[:, :, c2, :], a[:, 0:2 * HD].rearrange("p (g d) -> p g d", d=HD),
                                                    r, ALU.mult)
                    ins.then_inc(tok_ok, 1)
            for s in range(4 * NT + 1, 4 * NT + 8, 2):
                cc = (s - 4 * NT) // 2
                dve.wait_ge(acc_full, s + 1)
                dve.tensor_scalar((qbT if cc < 2 else kbT)[:, cc % 2, BANK:T], psum[:, 4 + s % 3, :],
                                  HD ** -0.5 if cc < 2 else 1.0, None, ALU.mult).then_inc(acc_dve, 1)

            kv3 = kvcT.rearrange("p (j s) -> p s j", s=CMP_STRIDE)
            dve.wait_ge(tokT_full, 4 * NT)
            dve.wait_ge(tokT_dve, 4 * NT)
            for hf in range(2):
                ins = dve.tensor_tensor(blk[:, 16 * hf:16 * hf + 16, 0:NC], kv3[:, :, hf:hf + NC],
                                        peT[:, 16 * hf:16 * hf + 16].unsqueeze(2).to_broadcast([P, 16, NC]), ALU.add)
            ins.then_inc(blk_ok, 1)
            dve.wait_ge(blk_ok, 1)
            own(dve.memset(v_cmp[:, :], 0.0))
            own(dve.memset(tmp_gv[:, :, :], 0.0))
            dve.wait_ge(hid_full, 1)
            own(dve.tensor_copy(tmp_gh[:, 0:128], psum[:, 0, 0:128]))
            own(dve.tensor_copy(tmp_gh[:, 128:256], psum[:, 1, 0:128]))
            own(dve.tensor_tensor(tmp_ge, tmp_gh, tmp_gh, ALU.mult))
            own(dve.tensor_scalar(tmp_ge, tmp_ge, 0.044715, 1.0, ALU.mult, ALU.add))
            own(dve.tensor_tensor(tmp_ge, tmp_ge, tmp_gh, ALU.mult))
            dve.tensor_scalar(tmp_ge, tmp_ge, -50.0, None, ALU.max).then_inc(gelu_in, 1)
            dve.wait_ge(gelu_e, 1)
            own(dve.tensor_scalar(tmp_ge, tmp_ge, 1.0, None, ALU.add))
            own(dve.reciprocal(tmp_ge, tmp_ge))
            own(dve.tensor_tensor(tmp_gh, tmp_gh, tmp_ge, ALU.mult))
            own(dve.memset(tmp_gh.rearrange("p (a j) -> p a j", a=4)[:, :, NC:NC + 1], 0.0))
            g4 = tmp_gh[:, 128:256].rearrange("p (c j) -> p c j", c=2)
            for i in range(2):
                ins = dve.tensor_copy(tmp_gv[:, :, i * 64:i * 64 + 64], g4)
            ins.then_inc(hid_ok, 1)
            copy_rows(4, late_row, 4, 4)
            dve.wait_ge(kcmp_full, 1)
            own(dve.tensor_copy(v_cmp[0:HD, 0:HD], psum[0:HD, 3, 0:HD]))
            own(dve.tensor_copy(v_cmp[HD:P, HD:P], psum[HD:P, 3, 0:HD]))
            dve.wait_ge(kcmp_rstd, 1)
            dve.tensor_scalar(sq[0:HD, 64:128], psum[0:HD, 2, 0:HD], stp[0:HD, 16:17], None, ALU.mult).then_inc(kcmp_tok, 1)
            dve.wait_ge(kcmpT_full, 1)
            dve.tensor_scalar(kcmpT[0:HD, :], psum[0:HD, 2, 0:HD], G_KC[0:HD, :], None, ALU.mult).then_inc(kcmp_ok, 1)

            own(scale_shift(mod_a2, mod_b2, psum[:, 7, 0:NK], psum[:, 7, NK:2 * NK], 4, 3, 2))
            dve.wait_ge(w_used, 10)
            v2 = ga_bc[:, :].rearrange("p (a d) -> p a d", a=2)
            own(dve.tensor_tensor(v2, psum[:, 4:6, :], v2, ALU.add))
            dve.wait_ge(w_used, 12)
            v2, b2 = (v.rearrange("p (a d) -> p a d", a=2) for v in (gm_bc[:, :], gm_bias))
            dve.tensor_tensor(v2, psum[:, 0:2, :], b2, ALU.add).then_inc(mod2_ok, 1)
            own(dve.memset(sel[:, :], 0.0))
            own(dve.memset(imp[:, :], 0.0))
            dve.wait_ge(mod2_ok, 1)
            dve.wait_ge(tables, 3)
            own(dve.tensor_scalar(st[:, 0:1], stp[:, 30:31], float(SEL_BLOCK), None, ALU.is_ge))
            own(dve.tensor_scalar(force[:, :, :], force[:, :, :], st[:, 0:1], None, ALU.subtract))
            xfa, xfb = zs[:, 0:NT * NSEL], zs[:, NT * NSEL:2 * NT * NSEL]
            ff = force[:, :, :].rearrange("p n b -> p (n b)")
            own(dve.tensor_scalar(xfa, ff, 0.0, MASKED, ALU.is_gt, ALU.mult))
            own(dve.tensor_scalar(xfb, ff, -1.0, FORCE, ALU.is_ge, ALU.mult))
            own(dve.scalar_tensor_tensor(xfb, ff, 0.0, xfb, ALU.is_le, ALU.mult))
            own(dve.tensor_tensor(ff, xfa, xfb, ALU.add))
            own(dve.tensor_scalar(force[:, :, 0:1], force[:, :, 0:1], FORCE, None, ALU.add))
            dve.wait_ge(sink_in, 16)
            gate4 = gates[:, :, :].rearrange("p n (h b) -> p n b h", b=3)

            def heads3(ap):
                return ap.rearrange("p (h d) -> p h d", d=HD)

            def bcast(ap, h):
                return ap.unsqueeze(2).to_broadcast([P, h, HD])

            def gather_output(n, what):
                if what == "cmp":
                    dve.wait_ge(pv_done, last_v[("cmp", n)] + 1)
                    if n:
                        dve.wait_ge(t_full, out_of[n - 1]["groups"][-1] + 1)
                    dve.tensor_tensor(heads3(o_tok[:, 0:A_W]), heads3(psum[:, 6, :]), bcast(gate4[:, n, 0, :], NSA_H),
                                      ALU.mult).then_inc(o_read, 1)
                    dve.wait_ge(o_read, 4 * n + 1)
                elif what == "win" or what == "slc":
                    i, b = (0, 7) if what == "win" else (1, 6)
                    dve.wait_ge(pv_done, last_v[(what, n)] + 1)
                    cf = coef[:, i * NSA_H:(i + 1) * NSA_H]
                    own(dve.reciprocal(cf, den[:, n % 2, i * NSA_H:(i + 1) * NSA_H]))
                    own(dve.tensor_tensor(cf, cf, gate4[:, n, 2 - i, :], ALU.mult))
                    dve.tensor_tensor(heads3(part), heads3(psum[:, b, :]), bcast(cf, NSA_H), ALU.mult).then_inc(o_read, 1)
                    dve.wait_ge(o_read, 4 * n + 2 + i)
                    own(dve.tensor_tensor(o_tok[:, 0:A_W], o_tok[:, 0:A_W], part, ALU.add))
                else:
                    dve.wait_ge(pv_done, max(last_v[("swa", n)], last_v[("sb", n)]) + 1)
                    cf = coef[:, 2 * NSA_H:]
                    own(dve.tensor_tensor(cf, den[:, n % 2, 2 * NSA_H:], sink_e[:, :], ALU.add))
                    own(dve.reciprocal(cf, cf))
                    own(dve.tensor_tensor(heads3(o_tok[:, A_W + B_W:]), heads3(psum[:, 7, 0:C_W]), bcast(cf, SWA_H),
                                          ALU.mult))
                    dve.tensor_copy(o_tok[:, A_W:A_W + B_W], psum[:, 7, C_W:]).then_inc(o_read, 1)

            for q, s in enumerate(slots):
                n, i, u = s["n"], s["i"], s["unit"]
                if u:
                    w, h = width(u), u["h"]
                    m1 = negm[:, q % 4:q % 4 + 1]
                    dve.wait_ge(s_full, u["s"] + 1)
                    if q >= 4:
                        dve.wait_ge(p_ok, q - 3)
                    if u["kind"] == "swa":
                        bias = swa_bias[:, h, 2 * P - w:2 * P]
                        own(dve.tensor_tensor_reduce(swa_s[h % 2][:, 0:w], score_buf(u)[:, 0:w], bias, 1.0, -3e38,
                                                     ALU.add, ALU.max, m1))
                        dve.tensor_scalar(m1, m1, sink[:, h:h + 1], -1.0, ALU.max, ALU.mult).then_inc(max_ok, 1)
                    else:
                        dve.tensor_reduce(m1, score_buf(u)[:, 0:w], AX.X, ALU.max, negate=True).then_inc(max_ok, 1)
                if "cmp" in s:
                    sc = score_buf(s["cmp"])[:, 0:BANK].rearrange("p (h c) -> p h c", h=NSA_H)
                    dve.wait_ge(s_full, s["cmp"]["s"] + 1)
                    own(dve.tensor_reduce(cmp_m[:, :], sc, AX.X, ALU.max))
                    own(dve.tensor_scalar(cmp_m[:, :], cmp_m[:, :], -1e26, None, ALU.max))
                    if n:
                        dve.wait_ge(cmp_e, n)
                    dve.tensor_tensor(cmp_s.rearrange("p (h c) -> p h c", h=NSA_H), sc,
                                      cmp_m[:, :].unsqueeze(2).to_broadcast([P, NSA_H, NC + 1]),
                                      ALU.subtract).then_inc(cmp_in, 1)
                if i == 1 and n < NT:
                    p3 = cmp_p.rearrange("p (h c) -> p h c", h=NSA_H)
                    dve.wait_ge(cmp_e, n + 1)
                    own(dve.tensor_reduce(cmp_r[:, :], p3, AX.X, ALU.add))
                    own(dve.tensor_scalar(cmp_r[:, :], cmp_r[:, :], 1e-30, None, ALU.max))
                    own(dve.reciprocal(cmp_r[:, :], cmp_r[:, :]))
                    dve.tensor_tensor(p3, p3, cmp_r[:, :].unsqueeze(2).to_broadcast([P, NSA_H, NC + 1]),
                                      ALU.mult).then_inc(cmp_pok, 1)
                if i == 2 and n < NT:
                    dve.wait_ge(cmp_pok, n + 1)
                    own(dve.tensor_reduce(imp[:, 1:NC + 2], cmp_p.rearrange("p (h c) -> p c h", h=NSA_H), AX.X, ALU.add))
                    own(dve.tensor_reduce(imp_b[:, 0, :], imp[:, 1:NC + 2].rearrange("p (b r) -> p b r", r=4)[:, :, 0:3],
                                          AX.X, ALU.add))
                    own(dve.tensor_tensor(imp_b[:, 1, :], imp[:, 0:NC + 1].rearrange("p (b r) -> p b r", r=4)[:, :, 0],
                                          imp[:, 1:NC + 2].rearrange("p (b r) -> p b r", r=4)[:, :, 3], ALU.add))
                    own(dve.scalar_tensor_tensor(imp_b[:, 0, :], imp_b[:, 1, :], 0.5, imp_b[:, 0, :], ALU.mult, ALU.add))
                if i == 3 and n < NT:
                    own(dve.tensor_tensor(imp_b[:, 0, :], imp_b[:, 0, :], force[:, n, :], ALU.add))
                    own(dve.max(top[:, :], imp_b[:, 0, :]))
                    own(dve.match_replace(imp_b[:, 1, :], top[:, :], imp_b[:, 0, :], TAKEN))
                    if n:
                        dve.wait_ge(t_full, sel_of[n - 1]["groups"][-1] + 1)
                    dve.tensor_scalar(sel[:, ROW_SEL:AUG], imp_b[:, 1, :], TAKEN_MIN, MASKED, ALU.is_lt,
                                      ALU.mult).then_inc(sel_ok, 1)
                if i == 2 and n:
                    gather_output(n - 1, "slc")
                    gather_output(n - 1, "rest")
                if i == 5 and n < NT:
                    gather_output(n, "cmp")
                if i == 10 and n < NT:
                    gather_output(n, "win")
                for t in s["T"]:
                    evacuate_groups(dve, t, 1)
                r, w, m = ride(q, 2)
                if r:
                    dve.wait_ge(sb_sp, m + 1)
                    dve.wait_ge(sb_ln, m + 1)
                    own(dve.tensor_tensor_scan(cum[:, 0:w][:, ::-1], zl[:, 0:w][:, ::-1], zc[:, 0:w][:, ::-1], 0.0,
                                               ALU.add, ALU.add))
                    dve.tensor_tensor(zs[:, 0:w], zs[:, 0:w], cum[:, 0:w], ALU.subtract).then_inc(sb_arg, 1)
                r, w, m = ride(q, 0)
                if r:
                    dve.wait_ge(sb_z, m + 1)
                    dve.tensor_scalar(zc[:, 0:w], zs[:, 0:w], 40.0, None, ALU.min).then_inc(sb_zc, 1)
            tokens_lo(dve, 0)
            weights_lo(dve, 0)
            tokens_lo(dve, 1)
            weights_lo(dve, 1)
            sums = 0
            for r in range(3 * 2 * NK):
                m, b, hf = r // 6, r // 2 % 3, r % 2
                y = yT[:, m, hf * BANK:(hf + 1) * BANK]
                if r % 2 == 0:
                    weights_lo(dve, r // 2 + 2)
                dve.wait_ge(mix_full, 2 * r + 2)
                dve.wait_ge(sig_ok, r + 1)
                if b == 0:
                    dve.tensor_tensor(y, sig[r % 2], psum[:, 2 * (r % 4) + 1, :], ALU.mult).then_inc(mix_done, 1)
                else:
                    if sums:
                        dve.wait_ge(y_ok, sums)
                    dve.tensor_tensor(gated, sig[r % 2], psum[:, 2 * (r % 4) + 1, :], ALU.mult).then_inc(mix_done, 1)
                    dve.wait_ge(mix_done, r + 1)
                    dve.tensor_tensor(y, y, gated, ALU.add).then_inc(y_ok, 1)
                    sums += 1
            for n in range(NT + 1):
                if n < NT:
                    dve.wait_ge(out_full, n + 1)
                    dve.wait_ge(xr_in[n % 2], 16 * (n // 2 + 1))
                    if n:
                        dve.wait_ge(xn2_ok, n)
                    t2 = x1[:, n, :].rearrange("p (a d) -> p a d", a=2)
                    own(dve.tensor_tensor(t2, psum[:, 2 * (n % 2):2 * (n % 2) + 2, :],
                                          ga_bc[:, :].rearrange("p (a d) -> p a d", a=2), ALU.mult))
                    dve.tensor_tensor(x1[:, n, :], x1[:, n, :], xr[n % 2], ALU.add).then_inc(x1_ok, 1)
                if n:
                    dve.wait_ge(xn2T_full, n)
                    for k in range(4):
                        ins = dve.tensor_scalar(h2T[:, k, :], psum[:, 4, k * P:(k + 1) * P], mod_a2[:, k:k + 1],
                                                mod_b2[:, k:k + 1], ALU.mult, ALU.add)
                    ins.then_inc(h2T_dve, 1)
                if n < NT:
                    dve.wait_ge(x1_rstd, n + 1)
                    if n:
                        dve.wait_ge(xn2_out, 16 * n)
                    dve.tensor_scalar(xn2, x1[:, n, :], stp[:, 1:2], None, ALU.mult).then_inc(xn2_ok, 1)
            score, val, t_a, oh1, oh2, t_b = r3[0], r3[1], r3[2], r3[3], r3[4], r3[5]
            dve.wait_ge(routing_tables, 1)
            dve.wait_ge(wr_in, 32)
            dve.wait_ge(score_ok, 1)
            own(dve.tensor_tensor(val, score, rbias[:, :].unsqueeze(1).to_broadcast([P, NT, NE]), ALU.add))
            v4 = val.rearrange("p n (g e) -> p (n g) e", g=N_GROUPS)
            NG8 = NT * N_GROUPS
            g_ = [route[6 + i // 4][:, (i % 4) * NG8:(i % 4 + 1) * NG8] for i in range(8)]
            own(dve.tensor_tensor(g_[0], v4[:, :, 0], v4[:, :, 1], ALU.max))
            own(dve.tensor_tensor(g_[1], v4[:, :, 2], v4[:, :, 3], ALU.max))
            own(dve.tensor_tensor(g_[2], v4[:, :, 0], v4[:, :, 1], ALU.add))
            own(dve.tensor_tensor(g_[3], v4[:, :, 2], v4[:, :, 3], ALU.add))
            own(dve.tensor_tensor(g_[0], g_[0], g_[1], ALU.add))
            own(dve.tensor_tensor(g_[0], g_[0], g_[2], ALU.max))
            own(dve.tensor_tensor(g_[0], g_[0], g_[3], ALU.max))
            g3 = [g.rearrange("p (n g) -> p n g", n=NT) for g in g_]
            red = [route[8][:, i * NT:(i + 1) * NT] for i in range(8)]

            def b3(ap, w):
                return ap.unsqueeze(2).to_broadcast([P, NT, w])

            def first_best(dst, src, tmp_, mx, w):
                own(dve.tensor_reduce(mx, src, AX.X, ALU.max))
                own(dve.tensor_tensor(tmp_, src, b3(mx, w), ALU.is_ge))
                own(dve.scalar_tensor_tensor(tmp_, tmp_, -100.0, iota_e[:, 0:w].unsqueeze(1).to_broadcast([P, NT, w]),
                                             ALU.mult, ALU.add))
                own(dve.tensor_reduce(mx, tmp_, AX.X, ALU.min))
                own(dve.tensor_tensor(dst, tmp_, b3(mx, w), ALU.is_equal))

            first_best(g3[4], g3[0], g3[1], red[0], N_GROUPS)
            own(dve.tensor_scalar(g_[4], g_[4], -MASKED, MASKED, ALU.mult, ALU.add))
            own(dve.tensor_tensor(v4, v4, g_[4].unsqueeze(2).to_broadcast([P, NG8, NE // N_GROUPS]), ALU.add))
            first_best(oh1, val, t_a, red[0], NE)
            own(dve.scalar_tensor_tensor(val, oh1, 2 * MASKED, val, ALU.mult, ALU.add))
            first_best(oh2, val, t_a, red[0], NE)
            dve.tensor_tensor(chosen[:, :].rearrange("p (n e) -> p n e", n=NT), oh1, oh2, ALU.add).then_inc(chosen_ok, 1)
            dve.wait_ge(rank_full, 1)
            pos, tot = r3[9], r3[10]
            own(dve.tensor_copy(route[9], psum[:, 7, 0:P]))
            own(dve.tensor_copy(route[10], psum[:, 7, P:2 * P]))
            run = r3[11]
            own(dve.memset(run[:, 0, :], 0.0))
            for n in range(1, NT):
                own(dve.tensor_tensor(run[:, n, :], run[:, n - 1, :], tot[:, n - 1, :], ALU.add))
            cnt = route[8][:, 64:64 + NE]
            own(dve.tensor_tensor(cnt, run[:, NT - 1, :], tot[:, NT - 1, :], ALU.add))
            t8 = route[2].rearrange("p (e m) -> p e m", e=NE)
            own(dve.tensor_tensor(t8, cnt.unsqueeze(2).to_broadcast([P, NE, NT]),
                                  iota_m[:, :].unsqueeze(1).to_broadcast([P, NE, NT]), ALU.is_gt))
            nb, base, last = plan_f[:, 0:NE], plan_f[:, NE:2 * NE], plan_f[:, 2 * NE:2 * NE + 1]
            ends, zero = route[8][:, 80:96], route[8][:, 96:112]
            own(dve.tensor_reduce(nb, t8, AX.X, ALU.add))
            own(dve.tensor_scalar(nb, nb, 1.0, None, ALU.max))
            own(dve.memset(zero, 0.0))
            own(dve.tensor_tensor_scan(ends, nb, zero, 0.0, ALU.add, ALU.add))
            own(dve.tensor_tensor(base, ends, nb, ALU.subtract))
            own(dve.tensor_copy(last, ends[:, NE - 1:NE]))
            own(dve.tensor_scalar(plan_f[:, 2 * NE + 1:2 * NE + 2], last, -1.0, float(N_BLK), ALU.mult, ALU.add))
            own(dve.tensor_copy(plan_i[:, :], plan_f[:, :]))
            own(dve.tensor_tensor(pos, pos, run, ALU.add))
            own(dve.scalar_tensor_tensor(pos, base.unsqueeze(1).to_broadcast([P, NT, NE]), float(P), pos,
                                         ALU.mult, ALU.add))
            for j, oh in enumerate((oh1, oh2)):
                own(dve.tensor_tensor(t_a, pos, oh, ALU.mult))
                own(dve.tensor_reduce(dest_f[:, j, :], t_a, AX.X, ALU.add))
            dve.tensor_copy(dest[:, :, :], dest_f[:, :, :]).then_inc(dest_ok, 1)
            for j, oh in enumerate((oh1, oh2)):
                own(dve.tensor_tensor(t_a, score, oh, ALU.mult))
                own(dve.tensor_reduce(w12[:, j, :], t_a, AX.X, ALU.add))
            own(dve.tensor_tensor(red[1], w12[:, 0, :], w12[:, 1, :], ALU.add))
            own(dve.reciprocal(red[1], red[1]))
            for j in range(2):
                own(dve.tensor_tensor(w12[:, j, :], w12[:, j, :], red[1], ALU.mult))
            def expert_tokens_dve(j):
                dve.wait_ge(xsT_half, j)
                for k in range(4):
                    ins = dve.tensor_scalar(xsT[:, k, :], psum[:, 2, k * P:(k + 1) * P], mod_a2[:, k:k + 1],
                                            mod_b2[:, k:k + 1], ALU.mult, ALU.add)
                ins.then_inc(xsT_dve, 1)

            expert_tokens_dve(1)
            dve.wait_ge(dest_ok, 1)
            n_blk = dve.value_load(plan_i[0:1, 2 * NE:2 * NE + 1], min_val=NE, max_val=N_BLK - 1)
            dve.nop().then_inc(a_ok, 1)
            dve.nop().then_inc(y_dve, 1)
            with dve.Fori(0, n_blk) as j:
                dve.wait_ge(silu_ok, j + 1)
                dve.wait_ge(up_full, j + 1)
                dve.tensor_tensor(act_a, silu_g, psum[:, 1, :], ALU.mult).then_inc(a_ok, 1)
                expert_tokens_dve(j + 2)
                dve.wait_ge(y_full, j + 1)
                dve.wait_ge(y_out, j * 16 + 16)
                dve.tensor_copy(y_sb[:, 0:BANK], psum[:, 5, :]).then_inc(y_dve, 1)
            for n in range(NT):
                dve.wait_ge(pair_in[n], 32)
                dve.wait_ge(scaled, n + 1)
                y1, y2 = pair[n]
                own(dve.scalar_tensor_tensor(y1, y2, w12[:, 1, n:n + 1], y1, ALU.mult, ALU.add))
                own(dve.tensor_tensor(res[n], y1, gm_bc[:, :], ALU.mult))
                dve.tensor_tensor(res[n], res[n], x1[:, n, :], ALU.add).then_inc(comb_ok, 1)

        @block.tensor
        def _(pe):
            def modulation(i0, bank, row_buf, before):
                def turn(r):
                    pe.wait_ge(row_ok, before + r + 1)
                    for j in range(4):
                        c = 4 * r + j
                        ins = pe.transpose(psum[:, 7, c:c + 1], row_buf(r)[:, j * P:(j + 1) * P], ident[0:1, 0:1])
                    ins.then_inc(turned, 1)

                for r in range(4):
                    wait_load(pe, i0 + r)
                    if r >= 2:
                        pe.wait_ge(row_ok, before + r - 1)
                    for k in range(NK):
                        mm = pe.matmul(psum[0:1, bank + r % 2, :], cond[:, k:k + 1], slot(slot_of(i0 + r))[:, k, :],
                                       start=(k == 0), stop=(k == NK - 1))
                    mm.then_inc(w_used, 1)
                    if r:
                        turn(r - 1)
                turn(3)

            pe.wait_ge(tables, 1)
            pe.wait_ge(small_in, 96)
            pe.transpose(psum[:, 7, 0:9 * NK], rows[:, :], ident[0:9 * NK, 0:9 * NK])
            pe.transpose(psum[:, 7, P:P + CMP_LEN], pe_rows[:, :], ident[0:CMP_LEN, 0:CMP_LEN]).then_inc(rowsT, 1)
            pe.wait_ge(cond_ok, 2)
            modulation(L_SC, 0, early_row, 0)

            for n in range(NT):
                pe.wait_ge(x_norm, n + 1)
                if n >= 2:
                    pe.wait_ge(hT_dve, n - 1)
                    pe.wait_ge(hT_act, n - 1)
                for k in range(NK):
                    ins = pe.transpose(psum[:, 2 * (n % 2) + k // 4, (k % 4) * P:(k % 4 + 1) * P],
                                       xt[n % 3][:, k * P:(k + 1) * P], ident[:, :])
                ins.then_inc(xT_full, 1)

            def transpose_heads(r):
                ch = r // NT
                t = tok[r % 2]
                pe.wait_ge(tok_ok, r + 1)
                if r >= 2:
                    pe.wait_ge(tokT_dve, r - 1)
                    pe.wait_ge(tokT_act, r - 1)
                b = [psum[:, 2 * (r % 2) + i, :] for i in range(2)]
                if ch == 0:
                    for h in range(NSA_H):
                        ins = pe.transpose(b[h // 4][0:HD + 1, (h % 4) * P:(h % 4 + 1) * P],
                                           t[:, h * (HD + 1):(h + 1) * (HD + 1)], ident[:, :])
                elif ch == 1:
                    pe.transpose(b[0][:, 0:P], t[:, 0:P], ident[:, :])
                    for i in range(2):
                        ins = pe.transpose(b[1][0:HD, i * P:(i + 1) * P], t[:, P + i * HD:P + (i + 1) * HD],
                                           ident[:, :])
                else:
                    for i in range(2):
                        ins = pe.transpose(b[i][:, 0:P], t[:, i * P:(i + 1) * P], ident[:, :])
                ins.then_inc(tokT_full, 1)

            pe.wait_ge(hT_dve, NT)
            pe.wait_ge(hT_act, NT)
            for s in range(4 * NT + 1):
                ch, n = divmod(s, NT)
                if s < 4 * NT:
                    w = TOKCH[ch][1]
                    if n == 0:
                        wait_load(pe, L_TOK + ch)
                    if s >= 3:
                        pe.wait_ge(squared, s - 2)
                        pe.wait_ge(tok_ok, s - 2)
                    for k in range(NK):
                        mm = pe.matmul(psum[:, 4 + s % 3, 0:w], hT[:, k, n * P:(n + 1) * P],
                                       slot(slot_of(L_TOK + ch))[:, k, 0:w], start=(k == 0), stop=(k == NK - 1))
                    mm.then_inc(acc_full, 1)
                if s:
                    transpose_heads(s - 1)
            wait_load(pe, L_QKB)
            for s in range(4 * NT, 4 * NT + 8):
                cc, hf = divmod(s - 4 * NT, 2)
                r = s - 3
                if r < 4 * NT:
                    pe.wait_ge(squared, r + 1)
                    pe.wait_ge(tok_ok, r + 1)
                else:
                    pe.wait_ge((acc_act, acc_dve)[r % 2], (r - 4 * NT) // 2 + 1)
                for k in range(NK):
                    mm = pe.matmul(psum[:, 4 + s % 3, :], slot(slot_of(L_QKB))[:, k, cc * P:(cc + 1) * P],
                                   hT[:, k, hf * BANK:(hf + 1) * BANK], start=(k == 0), stop=(k == NK - 1))
                mm.then_inc(acc_full, 1)

            for h in range(2):
                wait_load(pe, L_W1 + h)
            pe.wait_ge(blk_ok, 1)
            pe.wait_ge(tokT_act, 4 * NT)
            pe.wait_ge(tokT_dve, 4 * NT)
            for a in range(2):
                rs = slice(a * HD, (a + 1) * HD)
                for hc in range(2):
                    for l in range(CMP_LEN):
                        w = slot(slot_of(L_W1 + l // 16), k=16)
                        mm = pe.matmul(psum[:, a, hc * 64:hc * 64 + NC], w[rs, l % 16, hc * P:(hc + 1) * P],
                                       blk[rs, l, 0:NC], start=(l == 0), stop=(l == CMP_LEN - 1))
            mm.then_inc(hid_full, 1)

            pe.wait_ge(acc_act, 4)
            pe.wait_ge(acc_dve, 4)
            modulation(L_ADA2, 4, late_row, 4)

            pe.wait_ge(hid_ok, 1)
            for hc in range(2):
                pe.matmul(psum[0:64, 2, 0:HD], tmp_gh[:, hc * 64:(hc + 1) * 64], w2[:, 0, hc, :],
                          start=(hc == 0), stop=(hc == 1))
            for hc in range(2):
                mm = pe.matmul(psum[:, 3, 0:HD], tmp_gv[:, hc, :], w2[:, 1, hc, :], start=(hc == 0), stop=(hc == 1))
            mm.then_inc(kcmp_full, 1)

            for g in range(2):
                for h in range(2):
                    i = L_ADA2 + 4 + 2 * g + h
                    wait_load(pe, i)
                    for k in range(NK):
                        mm = pe.matmul(psum[:, (4, 0)[g] + h, :], cond_bc[:, k, :], slot(slot_of(i))[:, k, :],
                                       start=(k == 0), stop=(k == NK - 1))
                    mm.then_inc(w_used, 1)
                if g == 0:
                    pe.wait_ge(kcmp_tok, 1)
                    pe.transpose(psum[0:HD, 2, 0:64], sq[0:64, 64:128], ident[0:64, 0:64]).then_inc(kcmpT_full, 1)
            pe.wait_ge(mod2_ok, 1)
            pe.wait_ge(tables, 3)
            pe.wait_ge(kcmp_ok, 1)

            def scores(u):
                n, h, k = u["n"], u["h"], u["kind"]
                b = score_buf(u)
                if u["s"] >= 2:
                    wait_scores_read(pe, u["s"] - 2)
                if k == "cmp":
                    mask = stair[:, 56 - 8 * n:120 - 8 * n].unsqueeze(1).to_broadcast([P, NSA_H, 64])
                    pe.matmul(b[:, 0:BANK], identb[:, :], mask, start=True, stop=False)
                    for h in range(NSA_H):
                        mm = pe.matmul(b[:, h * 64:(h + 1) * 64], qaT[0:ROW_POS + 1, n, h, :], kcmpT[0:ROW_POS + 1, :],
                                       start=False, stop=(h == NSA_H - 1))
                    mm.then_inc(s_full, 1)
                    return
                w = width(u)
                if k in ("win", "slc"):
                    if "sel" in u:
                        wait_evacuated(pe, u["sel"]["groups"][0])
                    rows_k = ROW_POS + 1 if k == "win" else AUG
                    keys = (kwinT if k == "win" else kslcT)[0:rows_k, :]
                    lhs = qaT[0:rows_k, n, h, :]
                else:
                    rs = slice((h % 2) * HD, (h % 2 + 1) * HD)
                    keys = (kbT if k == "sb" else kcT)[rs, h // 2, :]
                    lhs = (qbT if k == "sb" else qcT)[rs, h // 2, n * P:(n + 1) * P]
                k0 = u["lo"] * P
                for c0 in range(0, w, BANK):
                    c1 = min(c0 + BANK, w)
                    masks = []
                    if k != "swa" and c1 == w:
                        masks.append((tri_strict if k == "sb" else tri_causal, w - P))
                    if k == "win" and n * P - k0 == NSA_WINDOW and c0 == 0:
                        masks.append((tri_low, 0))
                    mm = pe.matmul(b[:, c0:c1], lhs, keys[:, k0 + c0:k0 + c1], start=True, stop=not masks)
                    for j, (m, c) in enumerate(masks):
                        mm = pe.matmul(b[:, c:c + P], identb[:, :], m[:, :], start=False, stop=(j == len(masks) - 1))
                mm.then_inc(s_full, 1)

            def transposes(u):
                k, n = u["kind"], u["n"]
                if k == "cmp":
                    pe.wait_ge(cmp_pok, n + 1)
                    src = cmp_p
                elif k == "sel":
                    pe.wait_ge(sel_ok, n + 1)
                elif k == "out":
                    pe.wait_ge(o_read, 4 * n + 4)
                    src = o_tok
                elif k == "sb":
                    pe.wait_ge(pb_ok, n * SB_H + u["h"] + 1)
                    src = prob_b
                else:
                    pe.wait_ge(p_ok, u["slot"] + 1)
                    src = prob[u["slot"] % 2]
                for j, g in enumerate(u["groups"]):
                    bank, blocks = group(u, j)
                    if g >= 2:
                        wait_evacuated(pe, g - 2)
                    for c, t in enumerate(blocks):
                        if k == "sel":
                            ins = pe.transpose(bank[0:AUG, 0:P], sel[:, :], ident[:, :])
                        else:
                            ins = pe.transpose(bank[:, c * P:(c + 1) * P], src[:, t * P:(t + 1) * P], ident[:, :])
                    ins.then_inc(t_full, 1)

            def values(u):
                k, n, h = u["kind"], u["n"], u["h"]
                for g in u["groups"]:
                    wait_evacuated(pe, g)
                pt = probT[u["v"] % 2]
                if k == "cmp" and n:
                    pe.wait_ge(o_read, 4 * n - 1)
                elif k == "win" and n and h == 0:
                    pe.wait_ge(o_read, 4 * n)
                elif k == "slc" and h == 0:
                    pe.wait_ge(o_read, 4 * n + 1)
                elif k in ("sb", "swa") and h == 0:
                    pe.wait_ge(o_read, 4 * n + 2)
                if k == "cmp":
                    for g in range(NSA_H // 2):
                        mm = pe.matmul(psum[:, 6, g * P:(g + 1) * P], pt[:, g * P:(g + 1) * P], v_cmp[:, :],
                                       start=True, stop=True)
                    mm.then_inc(pv_done, 1)
                    return
                bank, c = {"win": (7, h), "slc": (6, h), "swa": (7, h), "sb": (7, SWA_H + h)}[k]
                for j in range(u["nb"]):
                    t = u["lo"] + j
                    if k in ("win", "slc"):
                        v = (v_win if k == "win" else v_slc)[:, t, :]
                    elif k == "swa":
                        v = v_c[:, t, (h // 2) * HD:(h // 2 + 1) * HD]
                    else:
                        v = v_b[:, t, h * HD:(h + 1) * HD]
                    mm = pe.matmul(psum[:, bank, c * HD:(c + 1) * HD], pt[:, j * P:(j + 1) * P], v,
                                   start=(j == 0), stop=(j == u["nb"] - 1))
                mm.then_inc(pv_done, 1)

            waiting = None
            for s in slots:
                for u in s["S"]:
                    scores(u)
                for u in s["T"]:
                    if waiting and "v" not in u:
                        values(waiting)
                        waiting = None
                    transposes(u)
                    if waiting:
                        values(waiting)
                    waiting = u if "v" in u else None
            if waiting:
                values(waiting)
            pe.wait_ge(o_read, 4 * NT)
            for g in (n_g - 2, n_g - 1):
                wait_evacuated(pe, g)
            for r in range(3 * 2 * NK):
                m, b, hf = r // 6, r // 2 % 3, r % 2
                s = slot_of(L_MIX + m)
                if r % 6 == 0:
                    wait_load(pe, L_MIX + m)
                if r >= 4:
                    pe.wait_ge(mix_done, r - 3)
                pe.wait_ge(w_rest, r // 2 + 1)
                if r < 2:
                    pe.wait_ge(h_rest, r + 1)
                for k in range(NK):
                    w_hi, w_lo = gate_hi(r // 2)[:, k, :], gate_lo(r // 2)[:, k, :]
                    t_hi, t_lo = (h[:, k, hf * BANK:(hf + 1) * BANK] for h in (h_hi, h_lo))
                    for i, (w, h) in enumerate(((w_lo, t_hi), (w_hi, t_lo), (w_hi, t_hi))):
                        mm = pe.matmul(psum[:, 2 * (r % 4), :], w, h, start=(k == 0 and i == 0),
                                       stop=(k == NK - 1 and i == 2))
                mm.then_inc(mix_full, 1)
                k0, k1 = ((0, 4), (4, 6), (6, 8))[b]
                for k in range(k0, k1):
                    mm = pe.matmul(psum[:, 2 * (r % 4) + 1, :], mix_branch(s)[:, k, :],
                                   oT[:, hf * 4:(hf + 1) * 4, k, :], start=(k == k0), stop=(k == k1 - 1))
                mm.then_inc(mix_full, 1)
            def router(n):
                for k in range(NK):
                    mm = pe.matmul(psum[:, 6, n * NE:(n + 1) * NE], h2T[:, k, :], wr[:, k, :],
                                   start=(k == 0), stop=(k == NK - 1))
                mm.then_inc(rt_full, 1)

            pe.wait_ge(y_ok, 4 * NK)
            for h in range(2):
                wait_load(pe, L_OUT + h)
            pe.wait_ge(wr_in, 32)
            for n in range(NT + 2):
                if n < NT:
                    if n >= 2:
                        pe.wait_ge(x1_ok, n - 1)
                    for h in range(2):
                        for k in range(NK):
                            mm = pe.matmul(psum[:, 2 * (n % 2) + h, :], yT[:, k, n * P:(n + 1) * P],
                                           slot(slot_of(L_OUT + h))[:, k, :], start=(k == 0), stop=(k == NK - 1))
                    mm.then_inc(out_full, 1)
                if 1 <= n <= NT:
                    pe.wait_ge(xn2_ok, n)
                    if n >= 2:
                        pe.wait_ge(h2T_act, n - 1)
                        pe.wait_ge(h2T_dve, n - 1)
                        router(n - 2)
                    for k in range(NK):
                        ins = pe.transpose(psum[:, 4 + k // 4, (k % 4) * P:(k % 4 + 1) * P], xn2[:, k * P:(k + 1) * P],
                                           ident[:, :])
                    ins.then_inc(xn2T_full, 1)
            pe.wait_ge(h2T_act, NT)
            pe.wait_ge(h2T_dve, NT)
            router(NT - 1)
            pe.wait_ge(routing_tables, 1)
            pe.wait_ge(chosen_ok, 1)
            pe.matmul(psum[:, 7, 0:P], before_b[:, :], chosen[:, :], start=True, stop=True)
            pe.matmul(psum[:, 7, P:2 * P], ones_b[:, :], chosen[:, :], start=True, stop=True).then_inc(rank_full, 1)

            def expert_tokens(half, full):
                for k in range(4 * half, 4 * half + 4):
                    ins = pe.transpose(psum[:, 2 + half, (k % 4) * P:(k % 4 + 1) * P], xs[:, k * P:(k + 1) * P],
                                       ident[:, :])
                ins.then_inc(full, 1)

            pe.nop().then_inc(xsT_full, 1)
            pe.wait_ge(xs_in, 16)
            expert_tokens(0, xsT_half)
            expert_tokens(1, xsT_full)
            with pe.Fori(0, NE // 2) as e2:
                for q in range(2):
                    e = pe.snap(e2 * 2 + q)
                    n_e = pe.value_load(plan_i[0:1, bass.ds(e, 1)], min_val=1, max_val=NT)
                    b_e = pe.value_load(plan_i[0:1, bass.ds(e + NE, 1)], min_val=0, max_val=N_BLK - 1)
                    with pe.Fori(0, n_e) as b:
                        j = pe.snap(b_e + b)
                        pe.wait_ge(xsT_act, j + 1)
                        pe.wait_ge(xsT_dve, j + 1)
                        pe.wait_ge(a_ok, j + 1)
                        for i, full in enumerate((gate_full, up_full)):
                            pe.wait_ge(expert_w[3 * q + i], e2 * 16 + 16)
                            for k in range(NK):
                                mm = pe.matmul(psum[:, i, :], xsT[:, k, :], slot(3 * q + i)[:, k, :],
                                               start=(k == 0), stop=(k == NK - 1))
                            mm.then_inc(full, 1)
                        pe.wait_ge(xs_in, j * 16 + 32)
                        expert_tokens(0, xsT_half)
                        pe.wait_ge(a_ok, j + 2)
                        for k in range(4):
                            ins = pe.transpose(psum[:, 4, k * P:(k + 1) * P], act_a[:, k * P:(k + 1) * P], ident[:, :])
                        ins.then_inc(aT_full, 1)
                        expert_tokens(1, xsT_full)
                        pe.wait_ge(aT_ok, j + 1)
                        pe.wait_ge(y_act, j + 1)
                        pe.wait_ge(y_dve, j + 1)
                        pe.wait_ge(expert_w[3 * q + 2], e2 * 16 + 16)
                        for h in range(2):
                            for k in range(4):
                                mm = pe.matmul(psum[:, 5 + h, :], aT[:, k, :],
                                               slot(3 * q + 2, k=4)[:, k, h * BANK:(h + 1) * BANK],
                                               start=(k == 0), stop=(k == 3))
                        mm.then_inc(y_full, 1)


def kernel(**inputs):
    import concourse.bacc as bacc
    from concourse.bass_utils import run_bass_kernel_spmd

    nc = bacc.Bacc("TRN2", target_bir_lowering=False, num_devices=1)
    arrays, args = {}, []
    for name in NAMES:
        a = np.ascontiguousarray(inputs[name])
        arrays[f"in_{name}_dram"] = a
        args.append(nc.dram_tensor(f"in_{name}_dram", a.shape, mybir.dt.from_np(a.dtype), kind="ExternalInput").ap())
    args.append(nc.dram_tensor("out_0_dram", inputs["x"].shape, F32, kind="ExternalOutput").ap())
    hybrid_trunk(nc, *args)
    return run_bass_kernel_spmd(nc, [arrays], core_ids=[0]).results[0]["out_0_dram"]
```
